# Optimizing a Trainium2 kernel written in Bass

```python
import jax, jax.numpy as jnp
from jax import lax
import numpy as np

D_MODEL = 2048
BATCH = 1
SEQ = 512
DEPTH = 1

W_CONV = D_MODEL // 2
CONV_GROUPS = 8
W_MLSTM = D_MODEL - W_CONV
N_HEADS_M = 4
HEAD_DIM_M = W_MLSTM // N_HEADS_M
CONV_WIDTH = 3
CHUNK = 64
D_FF = 5632
LN_EPS = 1e-5
HEAD_NORM_EPS = 1e-6
N_IN = 3 * W_CONV + 4 * W_MLSTM + 2 * N_HEADS_M

kernel_name = "hybrid_shortconv_mlstm_convffn_deepnorm"

def causal_dwconv(u, w, b=None):
    s = u.shape[1]
    up = jnp.pad(u, ((0, 0), (CONV_WIDTH - 1, 0), (0, 0)))
    y = w[0] * up[:, 0:s]
    for j in range(1, CONV_WIDTH):
        y = y + w[j] * up[:, j:j + s]
    return y if b is None else y + b

def layer_norm(x, g, b):
    xf = x.astype(jnp.float32)
    mu = jnp.mean(xf, axis=-1, keepdims=True)
    var = jnp.mean(jnp.square(xf - mu), axis=-1, keepdims=True)
    y = (xf - mu) * lax.rsqrt(var + LN_EPS) * g.astype(jnp.float32) + b.astype(jnp.float32)
    return y.astype(x.dtype)

def head_layer_norm(h, g):
    mu = jnp.mean(h, axis=-1, keepdims=True)
    var = jnp.mean(jnp.square(h - mu), axis=-1, keepdims=True)
    return (h - mu) * lax.rsqrt(var + HEAD_NORM_EPS) * g.astype(jnp.float32)

def mlstm_chunkwise(q, k, v, i_pre, f_pre):
    f32 = jnp.float32
    bsz, s, nh, dh = q.shape
    nc = s // CHUNK

    def to_chunks(t):
        return t.astype(f32).reshape(bsz, nc, CHUNK, nh, dh).transpose(1, 0, 3, 2, 4)

    def gate_chunks(t):
        return t.astype(f32).reshape(bsz, nc, CHUNK, nh).transpose(1, 0, 3, 2)

    qc = to_chunks(q) * (dh ** -0.5)
    kc = to_chunks(k)
    vc = to_chunks(v)
    ic = gate_chunks(i_pre)
    lfc = gate_chunks(jax.nn.log_sigmoid(f_pre.astype(f32)))
    causal = jnp.tril(jnp.ones((CHUNK, CHUNK), dtype=bool))

    def step(carry, xs):
        c_state, n_state, m_state = carry
        qb, kb, vb, ib, lfb = xs
        bcum = jnp.cumsum(lfb, axis=-1)
        g_tot = bcum[..., -1]
        log_d = bcum[..., :, None] - bcum[..., None, :] + ib[..., None, :]
        log_d = jnp.where(causal, log_d, -jnp.inf)
        inter_log = bcum + m_state[..., None]
        m_t = jnp.maximum(inter_log, jnp.max(log_d, axis=-1))
        d_w = jnp.exp(log_d - m_t[..., None])
        scores = jnp.einsum('bhtd,bhsd->bhts', qb, kb) * d_w
        inter_w = jnp.exp(inter_log - m_t)
        num = (jnp.einsum('bhts,bhse->bhte', scores, vb)
               + inter_w[..., None] * jnp.einsum('bhtd,bhde->bhte', qb, c_state))
        den = jnp.sum(scores, axis=-1) + inter_w * jnp.einsum('bhtd,bhd->bht', qb, n_state)
        h = num / jnp.maximum(jnp.abs(den), jnp.exp(-m_t))[..., None]
        w_log = g_tot[..., None] - bcum + ib
        m_new = jnp.maximum(g_tot + m_state, jnp.max(w_log, axis=-1))
        w = jnp.exp(w_log - m_new[..., None])
        decay = jnp.exp(g_tot + m_state - m_new)
        c_new = decay[..., None, None] * c_state + jnp.einsum('bhs,bhsd,bhse->bhde', w, kb, vb)
        n_new = decay[..., None] * n_state + jnp.einsum('bhs,bhsd->bhd', w, kb)
        return (c_new, n_new, m_new), h

    init = (jnp.zeros((bsz, nh, dh, dh), f32),
            jnp.zeros((bsz, nh, dh), f32),
            jnp.zeros((bsz, nh), f32))
    _, h = lax.scan(step, init, (qc, kc, vc, ic, lfc))
    return h.transpose(1, 0, 3, 2, 4).reshape(bsz, s, nh, dh)

def hybrid_mixer(x, w_in, b_gates, w_sc_conv, mh_gain, w_out):
    bsz, s, _ = x.shape
    proj = jnp.einsum('bsd,dn->bsn', x, w_in)
    splits = [W_CONV, 2 * W_CONV, 3 * W_CONV,
              3 * W_CONV + W_MLSTM, 3 * W_CONV + 2 * W_MLSTM,
              3 * W_CONV + 3 * W_MLSTM, 3 * W_CONV + 4 * W_MLSTM]
    c_b, c_c, c_h, q, k, v, o, gates = jnp.split(proj, splits, axis=-1)
    y_conv = c_b * causal_dwconv(c_c * c_h, w_sc_conv)
    gates = gates + b_gates
    i_pre, f_pre = gates[..., :N_HEADS_M], gates[..., N_HEADS_M:]
    hd = (bsz, s, N_HEADS_M, HEAD_DIM_M)
    h = mlstm_chunkwise(q.reshape(hd), k.reshape(hd), v.reshape(hd), i_pre, f_pre)
    h = head_layer_norm(h, mh_gain.reshape(N_HEADS_M, HEAD_DIM_M))
    h = jax.nn.sigmoid(o.astype(jnp.float32)).reshape(hd) * h
    y_mlstm = h.reshape(bsz, s, W_MLSTM).astype(x.dtype)
    y = jnp.concatenate([y_conv, y_mlstm], axis=-1)
    return jnp.einsum('bsd,de->bse', y, w_out)

def conv_ffn(x, w_up, w_ffn_conv, b_ffn_conv, w_down):
    hid = jnp.einsum('bsd,df->bsf', x, w_up)
    hid = causal_dwconv(hid, w_ffn_conv, b_ffn_conv)
    val, gate = hid[..., :D_FF], hid[..., D_FF:]
    return jnp.einsum('bsf,fd->bsd', jax.nn.silu(gate) * val, w_down)

def setup_inputs(seed: int = 0) -> dict:
    key = jax.random.key(seed)
    ks = jax.random.split(key, 16)
    beta = (8 * DEPTH) ** -0.25
    nrm = jax.random.normal
    x = nrm(ks[0], (BATCH, SEQ, D_MODEL), jnp.float32)
    col_scale = jnp.ones((N_IN,), jnp.float32)
    col_scale = col_scale.at[2 * W_CONV:3 * W_CONV].set(beta)
    col_scale = col_scale.at[3 * W_CONV + 2 * W_MLSTM:3 * W_CONV + 3 * W_MLSTM].set(beta)
    w_in = nrm(ks[1], (DEPTH, D_MODEL, N_IN), jnp.float32) * (D_MODEL ** -0.5) * col_scale
    b_i = 0.1 * nrm(ks[2], (DEPTH, N_HEADS_M), jnp.float32)
    b_f = jnp.linspace(3.0, 6.0, N_HEADS_M, dtype=jnp.float32) + 0.1 * nrm(ks[3], (DEPTH, N_HEADS_M), jnp.float32)
    b_gates = jnp.concatenate([b_i, b_f], axis=-1)
    w_sc_conv = nrm(ks[4], (DEPTH, CONV_WIDTH, W_CONV), jnp.float32) * (CONV_WIDTH ** -0.5)
    mh_gain = 1.0 + 0.02 * nrm(ks[5], (DEPTH, W_MLSTM), jnp.float32)
    w_out = nrm(ks[6], (DEPTH, D_MODEL, D_MODEL), jnp.float32) * (D_MODEL ** -0.5) * beta
    ln1_g = 1.0 + 0.02 * nrm(ks[7], (DEPTH, D_MODEL), jnp.float32)
    ln1_b = 0.02 * nrm(ks[8], (DEPTH, D_MODEL), jnp.float32)
    w_up = nrm(ks[9], (DEPTH, D_MODEL, 2 * D_FF), jnp.float32) * (D_MODEL ** -0.5)
    w_ffn_conv = nrm(ks[10], (DEPTH, CONV_WIDTH, 2 * D_FF), jnp.float32) * (CONV_WIDTH ** -0.5)
    b_ffn_conv = 0.02 * nrm(ks[11], (DEPTH, 2 * D_FF), jnp.float32)
    w_down = nrm(ks[12], (DEPTH, D_FF, D_MODEL), jnp.float32) * (D_FF ** -0.5) * beta
    ln2_g = 1.0 + 0.02 * nrm(ks[13], (DEPTH, D_MODEL), jnp.float32)
    ln2_b = 0.02 * nrm(ks[14], (DEPTH, D_MODEL), jnp.float32)
    return {"x": x, "w_in": w_in, "b_gates": b_gates, "w_sc_conv": w_sc_conv,
            "mh_gain": mh_gain, "w_out": w_out, "ln1_g": ln1_g, "ln1_b": ln1_b,
            "w_up": w_up, "w_ffn_conv": w_ffn_conv, "b_ffn_conv": b_ffn_conv,
            "w_down": w_down, "ln2_g": ln2_g, "ln2_b": ln2_b}

def reference(x, w_in, b_gates, w_sc_conv, mh_gain, w_out, ln1_g, ln1_b,
              w_up, w_ffn_conv, b_ffn_conv, w_down, ln2_g, ln2_b):
    alpha = (2 * DEPTH) ** 0.25
    for l in range(DEPTH):
        mix = hybrid_mixer(x, w_in[l], b_gates[l], w_sc_conv[l], mh_gain[l], w_out[l])
        x = layer_norm(alpha * x + mix, ln1_g[l], ln1_b[l])
        ff = conv_ffn(x, w_up[l], w_ffn_conv[l], b_ffn_conv[l], w_down[l])
        x = layer_norm(alpha * x + ff, ln2_g[l], ln2_b[l])
    return x


_drawn_inputs = setup_inputs


def setup_inputs(seed=0):
    import zlib

    import numpy as np

    out = dict(_drawn_inputs(seed))
    spreads = {}
    factors = {'mh_gain': 21.367,
     'ln1_g': 2.709,
     'ln1_b': 2.721,
     'b_ffn_conv': 6.774,
     'ln2_g': 7.7,
     'ln2_b': 7.74}
    for name, (base, spread) in spreads.items():
        noise = np.random.default_rng([zlib.crc32(name.encode()), seed]).standard_normal(out[name].shape)
        drawn = base * np.exp(spread * noise) if base else spread * noise
        out[name] = __import__('jax').numpy.asarray(drawn.astype(out[name].dtype))
    for name, factor in factors.items():
        out[name] = (out[name] * factor).astype(out[name].dtype)
    return out
```

```python
from contextlib import ExitStack

import concourse.bass as bass
from concourse import mybir

F32 = mybir.dt.float32
F32R = mybir.dt.float32r
ALU = mybir.AluOpType
ACT = mybir.ActivationFunctionType

P = 128
SEQ, D, W_CONV, W_ML, D_FF = 512, 2048, 1024, 1024, 5632
HEADS = 4
HD = W_ML // HEADS
TW = 2048
KD = D // P
NS = SEQ // P
ALPHA = 2.0 ** 0.25
LN_EPS, HEAD_EPS = 1e-5, 1e-6
Q_SCALE = float(HD) ** -0.5
RAW, SPLIT = 3, 2
FCH = 4
GROUPS = D_FF // P // FCH
BODY = 3 * FCH

MIX = [("gates",)]
for _pair in range(HEADS // 2):
    MIX += [("v", _pair, q) for q in range(4)] + [("o", _pair, q) for q in range(4)]
    MIX += [("qk", 2 * _pair + s, j) for s in range(2) for j in range(4)]
MIX += [("conv", c, j) for c in range(W_CONV // P) for j in range(3)]
N_MIX = len(MIX)
N_OUT = 2 * KD
OUT0 = N_MIX
FF0 = N_MIX + N_OUT
CONV0 = MIX.index(("conv", 0, 0))
CONV_PEELED = 2
CONV_LOOP0 = CONV0 + 3 * CONV_PEELED
CONV_TURNS = (W_CONV // P - CONV_PEELED) // 2
assert CONV_LOOP0 % RAW == 0 and FF0 % RAW == 2 and BODY % 6 == 0
LAST_QK = {MIX.index(("qk", h, 3)): h for h in range(HEADS)}
B_O, B_S, B_V = 0, 2, 4
SC_AT = [0, 512, 896, 1152]
SC_W = [SEQ - P * j for j in range(NS)]
SC_ALL = sum(SC_W)
Y_CONV = 4096
G_X0, G_X1, G_T1, G_T2 = Y_CONV, Y_CONV + 768, Y_CONV + 1536, Y_CONV + 2048
HN_AT = Y_CONV + 1792
SC_BUF = Y_CONV + 4096 - SC_ALL


def build(nc, x_t, x_rows, w_mix, w_out, w_up, w_down, b_gates, conv_w, gain, ln1_cols, ffn_conv,
          ln1_rows, ln2_rows, ident_in, head_rows_in, causal_in, out):
    ctx = ExitStack()
    with ctx:
        def sb(name, shape, dt=F32, scope=ctx):
            return scope.enter_context(nc.sbuf_tensor(name, shape, dt))

        def sem(name):
            return ctx.enter_context(nc.semaphore(name))

        raw = sb("raw", [P, RAW, TW])
        w_hi = sb("w_hi", [P, SPLIT, TW], F32R)
        w_lo = sb("w_lo", [P, SPLIT, TW], F32R)
        act_hi = sb("act_hi", [P, 2, KD, 256], F32R)
        act_lo = sb("act_lo", [P, 2, KD, 256], F32R)
        stream = sb("stream", [P, NS * D])
        ident = sb("ident", [P, P])
        causal = sb("causal", [P, P])
        head_rows = sb("head_rows", [HEADS, HEADS, P])
        bg = sb("bg", [HEADS, 2])
        cw = sb("cw", [P, 8, 3])
        gain_c = sb("gain_c", [P, 8])
        ln1_c = sb("ln1_c", [P, 2, KD])
        fc = sb("fc", [P, 2 * D_FF // P * 4])
        gate_cols = sb("gate_cols", [P, 2, NS, HEADS])
        den = sb("den", [P, 4, NS])
        bstat = sb("bstat", [P, NS, 4, 6])
        mv = sb("mv", [P, NS, 2])
        std = sb("std", [P, NS])
        rstd = sb("rstd", [P, NS])
        eps = sb("eps", [P, 2])
        uc = sb("uc", [P, 2 + SEQ])
        ut = sb("ut", [P, SEQ])
        ux = sb("ux", [P, SEQ])
        with ExitStack() as stage:
            v_hi = sb("v_hi", [P, NS, 2, HD + 2], F32R, stage)
            v_lo = sb("v_lo", [P, NS, 2, HD + 2], F32R, stage)
            qk_hi = sb("qk_hi", [P, 4, SEQ], F32R, stage)
            qk_lo = sb("qk_lo", [P, 4, SEQ], F32R, stage)
            p_hi = sb("p_hi", [P, SC_ALL], F32R, stage)
            p_lo = sb("p_lo", [P, SC_ALL], F32R, stage)
        with ExitStack() as stage:
            ym_hi = sb("ym_hi", [P, 8, SEQ], F32R, stage)
            ym_lo = sb("ym_lo", [P, 8, SEQ], F32R, stage)
        with ExitStack() as stage:
            h_hi = sb("h_hi", [P, FCH, SEQ], F32R, stage)
            h_lo = sb("h_lo", [P, FCH, SEQ], F32R, stage)
            x1_full = sb("x1_full", [P, 4, SEQ], F32, stage)
            f_val, f_gate, f_silu, f_prod = (x1_full[:, j, :] for j in range(4))
            ln_rows = sb("ln_rows", [P, 2, D], F32, stage)
        ps = ctx.enter_context(nc.psum_tensor("ps", [P, 8, 512], F32))

        g_x0, g_x1 = (stream[0:HEADS, g:g + 768] for g in (G_X0, G_X1))
        g_t1, g_t2 = (stream[0:HEADS, g:g + 512] for g in (G_T1, G_T2))
        hn = stream[:, HN_AT:HN_AT + NS * HD].rearrange("p (c e) -> p c e", c=NS)
        sc = stream[:, SC_BUF:SC_BUF + SC_ALL]
        y_ml = stream[:, 0:4096].rearrange("p (c e) -> p c e", c=NS)
        y_cv = stream[:, Y_CONV:Y_CONV + 4096].rearrange("p (k t) -> p k t", k=8)
        x_raw = stream[:, :].rearrange("p (k t) -> p k t", k=KD)
        rows = stream[:, :].rearrange("p (c n) -> p c n", c=NS)

        consts_in = sem("consts_in")
        x_in = [sem(f"x_in{i}") for i in range(4)]
        raw_in = [sem(f"raw_in{i}") for i in range(RAW)]
        res_in = [sem(f"res_in{i}") for i in range(2)]
        ln1_in = sem("ln1_in")
        ln2_in = sem("ln2_in")
        x_hi, x_lo = sem("x_hi"), sem("x_lo")
        tile_hi, tile_lo, tile_done = sem("tile_hi"), sem("tile_lo"), sem("tile_done")
        pads = sem("pads")
        gate_dve, gate_act = sem("gate_dve"), sem("gate_act")
        gates_ready, gate_turned, gate_cols_ready = sem("gates_ready"), sem("gate_turned"), sem("gate_cols_ready")
        vp_hi, vp_lo, o_sig = sem("vp_hi"), sem("vp_lo"), sem("o_sig")
        qk_h, qk_l = sem("qk_h"), sem("qk_l")
        g_spread, decay_arg, decay_exp, decay_ready = sem("g_spread"), sem("decay_arg"), sem("decay_exp"), sem("decay_ready")
        scores_done, p_raw, p_h, p_l = sem("scores_done"), sem("p_raw"), sem("p_h"), sem("p_l")
        pv_done, norm_step, head_read = sem("pv_done"), sem("norm_step"), sem("head_read")
        head_var, head_std, y_ready = sem("head_var"), sem("head_std"), sem("y_ready")
        y_turned, ym_h, ym_l = sem("y_turned"), sem("ym_h"), sem("ym_l")
        conv_c, conv_u, conv_step, conv_y = sem("conv_c"), sem("conv_u"), sem("conv_step"), sem("conv_y")
        yc_h, yc_l = sem("yc_h"), sem("yc_l")
        z_ready, ln_step, ln_var, ln_std, zn_ready = sem("z_ready"), sem("ln_step"), sem("ln_var"), sem("ln_std"), sem("zn_ready")
        x1_turned, x1_full_s, x1_h, x1_l = sem("x1_turned"), sem("x1_full_s"), sem("x1_h"), sem("x1_l")
        rstd_step = sem("rstd_step")
        pool_step, res_ready = sem("pool_step"), sem("res_ready")
        ff_step, ff_conv, silu_done, prod_ready = sem("ff_step"), sem("ff_conv"), sem("silu_done"), sem("prod_ready")
        h_h, h_l, down_done, added = sem("h_h"), sem("h_l"), sem("down_done"), sem("added")
        gained, out_ready, stored = sem("gained"), sem("out_ready"), sem("stored")

        block = ctx.enter_context(nc.Block())

        def conv_terms(eng, dst, src, pars, step, count):
            eng.tensor_scalar(dst[:, :], src[:, :], pars[2], pars[3], ALU.mult, ALU.add).then_inc(step, 1)
            for lag in (1, 2):
                eng.wait_ge(step, count + lag)
                last = eng.scalar_tensor_tensor(dst[:, lag:SEQ], src[:, 0:SEQ - lag], pars[2 - lag],
                                                dst[:, lag:SEQ], ALU.mult, ALU.add)
                if lag == 1:
                    last.then_inc(step, 1)
            return last

        @block.sync
        def _(sp):
            def load(src, n, s):
                if not (isinstance(n, int) and n < RAW):
                    sp.wait_ge(tile_lo, n - RAW + 1)
                sp.dma_start(raw[:, s % RAW, :], src).then_inc(raw_in[s % RAW], 16)

            def load_x(i):
                sp.dma_start(x_raw[:, 4 * i:4 * i + 4, :], x_t[4 * i:4 * i + 4].rearrange("k p t -> p k t")
                             ).then_inc(x_in[i], 16)

            load_x(0)
            load(w_mix[0], 0, 0)
            load_x(1)
            for dst, src in ((ident[:, :], ident_in), (causal[:, :], causal_in), (bg[:, :], b_gates),
                             (head_rows[:, :, :], head_rows_in), (cw[:, :, :], conv_w), (gain_c[:, :], gain),
                             (ln1_c[:, :, :], ln1_cols), (fc[:, :], ffn_conv)):
                sp.dma_start(dst, src).then_inc(consts_in, 16)
            load_x(2)
            load_x(3)
            for n in range(1, CONV_LOOP0):
                load(w_mix[n], n, n)
            with sp.Fori(0, CONV_TURNS) as i:
                for j in range(6):
                    load(w_mix[bass.ds(i * 6 + (CONV_LOOP0 + j), 1)].rearrange("o p n -> (o p) n"),
                         i * 6 + (CONV_LOOP0 + j), CONV_LOOP0 + j)
            for i in range(N_OUT):
                k = i % KD
                r = W_CONV + k * P if k < 8 else (k - 8) * P
                load(w_out[r:r + P, :], OUT0 + i, OUT0 + i)
                if i == 5:
                    sp.wait_ge(y_turned, 8)
                    sp.dma_start(rows[:, 0:2, :], x_rows[0:2].rearrange("c p n -> p c n")).then_inc(res_in[0], 16)
                if i == KD:
                    sp.wait_ge(yc_l, 8)
                    sp.dma_start(rows[:, 2:4, :], x_rows[2:4].rearrange("c p n -> p c n")).then_inc(res_in[1], 16)
            load(w_up[0], FF0, FF0)
            sp.wait_ge(tile_done, FF0)
            for r in range(2):
                sp.dma_start(ln_rows[:, r, :], ln1_rows[r].partition_broadcast(P)).then_inc(ln1_in, 16)

            def group(i, last):
                for j in range(7 if last else 8):
                    src = w_up[8 * i + 1 + j] if last else w_up[bass.ds(i * 8 + (1 + j), 1)].rearrange("o p n -> (o p) n")
                    load(src, i * BODY + (FF0 + 1 + j), j)
                for j in range(4):
                    at = (7 if last else 8) + j
                    src = w_down[4 * i + j] if last else w_down[bass.ds(i * 4 + j, 1)].rearrange("o p n -> (o p) n")
                    load(src, i * BODY + (FF0 + 1 + at), at)

            with sp.Fori(0, GROUPS - 1) as i:
                group(i, False)
            group(GROUPS - 1, True)
            sp.wait_ge(res_ready, NS)
            for r in range(2):
                sp.dma_start(ln_rows[:, r, :], ln2_rows[r].partition_broadcast(P)).then_inc(ln2_in, 16)
            for c in range(NS):
                sp.wait_ge(out_ready, c + 1)
                sp.dma_start(out[c * P:(c + 1) * P, :], rows[:, c, :]).then_inc(stored, 16)
            sp.wait_ge(stored, 16 * NS)

        @block.gpsimd
        def _(pool):
            pool.memset(v_hi[:, :, :, HD:HD + 2].bitcast(F32), 1.0).then_inc(pads, 1)
            pool.memset(uc[:, 0:2], 0.0).then_inc(pads, 1)
            pool.memset(v_lo[:, :, :, HD:HD + 2].bitcast(F32), 0.0).then_inc(pads, 1)
            pool.memset(eps[:, 0:1], HEAD_EPS).then_inc(pads, 1)
            pool.memset(eps[:, 1:2], LN_EPS).then_inc(pads, 1)
            pool.wait_ge(ln1_in, 32)
            pool.tensor_scalar(ln_rows[:, :, :], ln_rows[:, :, :], ALPHA, None, ALU.mult).then_inc(pool_step, 1)
            for k in range(KD):
                pool.wait_ge(x1_h, k + 1)
                pool.tensor_tensor(act_lo[:, :, k, :], x1_full[:, k % 4, :].rearrange("p (a t) -> p a t", a=2),
                                   act_hi[:, :, k, :].bitcast(F32), ALU.subtract).then_inc(x1_l, 1)
            pool.wait_ge(x1_turned, KD)
            pool.wait_ge(pool_step, 1)
            for c in range(NS):
                pool.tensor_tensor(rows[:, c, :], rows[:, c, :], ln_rows[:, 0, :], ALU.mult).then_inc(pool_step, 1)
                pool.wait_ge(pool_step, c + 2)
                pool.tensor_tensor(rows[:, c, :], rows[:, c, :], ln_rows[:, 1, :], ALU.add).then_inc(res_ready, 1)
            for c in range(NS):
                pool.wait_ge(gained, c + 1)
                pool.tensor_tensor(rows[:, c, :], rows[:, c, :], ln_rows[:, 1, :], ALU.add).then_inc(out_ready, 1)

        @block.scalar
        def _(act):
            def split(n, s, third):
                act.wait_ge(raw_in[s % RAW], third * 16 + 16)
                if not (isinstance(n, int) and n < SPLIT):
                    act.wait_ge(tile_done, n - SPLIT + 1)
                act.activation(w_hi[:, s % SPLIT, :], raw[:, s % RAW, :], ACT.Copy).then_inc(tile_hi, 1)

            def split_x(k):
                if k % 4 == 0:
                    act.wait_ge(x_in[k // 4], 16)
                act.activation(act_hi[:, :, k, :], x_raw[:, k, :].rearrange("p (a t) -> p a t", a=2),
                               ACT.Copy).then_inc(x_hi, 1)

            def mix_work(n):
                kind = MIX[n]
                h = LAST_QK.get(n)
                if n == 0:
                    act.wait_ge(gate_dve, 5)
                    act.activation(g_x1[:, 256:768], g_x1[:, 256:768], ACT.Exp, scale=-1.0).then_inc(gate_act, 1)
                    act.wait_ge(gate_act, 1)
                    act.activation(g_x1[:, 256:768], g_x1[:, 256:768], ACT.Ln, bias=1.0).then_inc(gate_act, 1)
                if n == 5:
                    act.wait_ge(gate_dve, 28)
                    act.activation(g_t2, g_t2, ACT.Exp, scale=-1.0).then_inc(gate_act, 1)
                if kind[0] == "v" and kind[2] == 3:
                    act.wait_ge(tile_done, n + 1)
                    if kind[1]:
                        act.wait_ge(pv_done, 2 * NS * kind[1])
                    for c in range(NS):
                        act.activation(v_hi[:, c, :, 0:HD], ps[:, B_V + c, :].rearrange("p (h e) -> p h e", h=2),
                                       ACT.Copy).then_inc(vp_hi, 1)
                if kind[0] == "o" and kind[2] == 3:
                    act.wait_ge(tile_done, n + 1)
                    for c in range(NS):
                        act.activation(y_ml[:, c, kind[1] * 512:kind[1] * 512 + 512], ps[:, B_O + c, :],
                                       ACT.Sigmoid).then_inc(o_sig, 1)
                if kind[0] == "qk":
                    act.wait_ge(tile_done, n + 1)
                    act.wait_ge(scores_done, NS * kind[1]) if kind[1] else None
                    act.activation(qk_hi[:, kind[2], :], ps[:, B_V + kind[2], :], ACT.Copy).then_inc(qk_h, 1)
                if h is not None:
                    act.wait_ge(decay_arg, h + 1)
                    act.activation(sc, sc, ACT.Exp, scale=-1.0).then_inc(decay_exp, 1)
                if n - 1 in LAST_QK:
                    h = LAST_QK[n - 1]
                    act.wait_ge(p_raw, NS * (h + 1))
                    if h:
                        act.wait_ge(pv_done, NS * h)
                    act.activation(p_hi[:, :], sc, ACT.Copy).then_inc(p_h, 1)
                if n - 2 in LAST_QK:
                    act.wait_ge(head_var, LAST_QK[n - 2] + 1)
                    act.activation(std[:, :], mv[:, :, 1], ACT.Sqrt, bias=eps[:, 0:1]).then_inc(head_std, 1)

            def conv_work(chunk, part):
                if part == 0:
                    act.wait_ge(tile_done, chunk * 3 + (CONV0 + 1))
                    if not isinstance(chunk, int) or chunk > 0:
                        act.wait_ge(conv_u, chunk)
                    act.activation(ux[:, :], ps[:, B_V, :], ACT.Copy).then_inc(conv_c, 1)

            def turn_y(m):
                act.wait_ge(y_turned, m + 1)
                act.activation(ym_hi[:, m, :], ps[:, m % 4, :], ACT.Copy, scale=gain_c[:, m:m + 1]).then_inc(ym_h, 1)

            act.wait_ge(x_in[0], 16)
            for k in range(4):
                split_x(k)
            split(0, 0, 0)
            for k in range(4, KD):
                split_x(k)
            split(1, 1, 0)
            act.wait_ge(consts_in, 16 * 8)
            act.wait_ge(pads, 5)
            for n in range(CONV_LOOP0):
                split(n + 2, n + 2, (n + 2) // 3)
                if n >= CONV0:
                    if n - 1 in LAST_QK or n - 2 in LAST_QK:
                        mix_work(n)
                    conv_work(*MIX[n][1:])
                else:
                    mix_work(n)
                if n == CONV_LOOP0 - 2:
                    for m in range(4):
                        turn_y(m)
                if n == CONV_LOOP0 - 1:
                    for m in range(4, 8):
                        turn_y(m)
            with act.Fori(0, CONV_TURNS) as i:
                for j in range(6):
                    split(i * 6 + (CONV_LOOP0 + j + 2), CONV_LOOP0 + j + 2, i * 2 + (CONV_LOOP0 + j + 2) // 3)
                    conv_work(i * 2 + (CONV_PEELED + j // 3), j % 3)
            def ln_sqrt(done, first, last):
                act.wait_ge(ln_var, done)
                act.activation(std[:, first:last], mv[:, first:last, 1], ACT.Sqrt, bias=eps[:, 1:2]).then_inc(ln_std, 1)

            for i in range(N_OUT - 1):
                n = OUT0 + i + 2
                split(n, n, n // 3)
                if i == KD + 1:
                    ln_sqrt(1, 0, 2)
                if i < 8:
                    act.wait_ge(tile_done, OUT0)
                    act.wait_ge(conv_y, 8)
                    act.activation(act_hi[:, :, i, :], y_cv[:, i, :].rearrange("p (a t) -> p a t", a=2),
                                   ACT.Copy).then_inc(yc_h, 1)
            ln_sqrt(2, 2, 4)
            for k in range(KD):
                act.wait_ge(x1_full_s, k + 1)
                act.activation(act_hi[:, :, k, :], x1_full[:, k % 4, :].rearrange("p (a t) -> p a t", a=2),
                               ACT.Copy).then_inc(x1_h, 1)

            def hidden(i, pair):
                act.wait_ge(ff_conv, i * 8 + (2 * pair + 2))
                act.activation(f_silu[:, :], f_gate[:, :], ACT.Silu).then_inc(silu_done, 1)
                act.wait_ge(prod_ready, i * 4 + (pair + 1))
                act.activation(h_hi[:, pair, :], f_prod[:, :], ACT.Copy).then_inc(h_h, 1)

            def group(i, last):
                for j in range(BODY - last):
                    if not (last and j == BODY - 2):
                        s = j + 1
                        split(i * BODY + (FF0 + 1 + s), s, i * 4 + (FF0 + 1 + s) // 3)
                    if j < 7 and j % 2 == 0:
                        hidden(i, j // 2)
            split(FF0 + 1, 0, (FF0 + 1) // 3)
            with act.Fori(0, GROUPS - 1) as i:
                group(i, False)
            group(GROUPS - 1, True)
            for c in range(NS):
                ln_sqrt(3 + c, c, c + 1)

        @block.vector
        def _(dve):
            def split(n, s):
                dve.wait_ge(tile_hi, n + 1)
                dve.tensor_tensor(w_lo[:, s % SPLIT, :], raw[:, s % RAW, :], w_hi[:, s % SPLIT, :].bitcast(F32),
                                  ALU.subtract).then_inc(tile_lo, 1)

            def split_x(k):
                dve.wait_ge(x_hi, k + 1)
                dve.tensor_tensor(act_lo[:, :, k, :], x_raw[:, k, :].rearrange("p (a t) -> p a t", a=2),
                                  act_hi[:, :, k, :].bitcast(F32), ALU.subtract).then_inc(x_lo, 1)

            def doubling(first, last, op, count):
                for s in range(first, last):
                    src, dst = (g_x0, g_x1) if s % 2 == 0 else (g_x1, g_x0)
                    dve.wait_ge(gate_dve, count + s - first)
                    dve.tensor_tensor(dst[:, 256:768], src[:, 256:768], src[:, 256 - 2 ** s:768 - 2 ** s],
                                      op).then_inc(gate_dve, 1)

            def gates_a():
                dve.wait_ge(consts_in, 16 * 8)
                dve.wait_ge(tile_done, 1)
                dve.tensor_scalar(g_t1, ps[0:HEADS, 0, :], bg[:, 0:1], None, ALU.add).then_inc(gate_dve, 1)
                dve.tensor_copy(g_t2, ps[32:32 + HEADS, 0, :]).then_inc(gate_dve, 1)
                dve.memset(g_x0[:, 0:256], 0.0)
                dve.memset(g_x1[:, 0:256], 0.0).then_inc(gate_dve, 1)
                dve.wait_ge(gate_dve, 2)
                dve.tensor_scalar(g_t2, g_t2, bg[:, 1:2], None, ALU.add).then_inc(gate_dve, 1)
                dve.wait_ge(gate_dve, 4)
                dve.scalar_tensor_tensor(g_x1[:, 256:768], g_t2, -1.0, g_t2, ALU.mult, ALU.max).then_inc(gate_dve, 1)

            def gates_b():
                dve.wait_ge(gate_act, 2)
                dve.scalar_tensor_tensor(g_x0[:, 256:768], g_t2, 0.0, g_x1[:, 256:768], ALU.min,
                                         ALU.subtract).then_inc(gate_dve, 1)

            def gates_mid():
                dve.wait_ge(gate_dve, 15)
                dve.tensor_tensor(g_t1, g_t1, g_x1[:, 256:768], ALU.subtract).then_inc(gate_dve, 1)
                dve.tensor_copy(g_t2, g_x1[:, 256:768]).then_inc(gate_dve, 1)
                dve.wait_ge(gate_dve, 16)
                dve.tensor_copy(g_x0[:, 256:768], g_t1).then_inc(gate_dve, 1)

            def norm_heads(h):
                t = h * 13
                dve.wait_ge(pv_done, NS * (h + 1))
                dve.tensor_copy(den[:, 0, :], ps[:, 0:NS, HD]).then_inc(norm_step, 1)
                dve.wait_ge(norm_step, t + 1)
                dve.scalar_tensor_tensor(den[:, 1, :], den[:, 0, :], -1.0, den[:, 0, :], ALU.mult,
                                         ALU.max).then_inc(norm_step, 1)
                dve.wait_ge(norm_step, t + 2)
                dve.tensor_tensor(den[:, 2, :], den[:, 1, :], gate_cols[:, 1, :, h], ALU.max).then_inc(norm_step, 1)
                dve.wait_ge(norm_step, t + 3)
                dve.reciprocal(den[:, 3, :], den[:, 2, :]).then_inc(norm_step, 1)
                dve.wait_ge(norm_step, t + 4)
                for c in range(NS):
                    dve.tensor_scalar(hn[:, c, :], ps[:, c, 0:HD], den[:, 3, c:c + 1], None,
                                      ALU.mult).then_inc(head_read, 1)
                for c in range(NS):
                    dve.wait_ge(head_read, NS * h + c + 1)
                    dve.bn_stats(bstat[:, c, 0, :], hn[:, c, :]).then_inc(norm_step, 1)
                for c in range(NS):
                    dve.wait_ge(norm_step, t + 5 + c)
                    last = dve.bn_aggr(mv[:, c, :], bstat[:, c, 0, :])
                last.then_inc(head_var, 1)
                dve.wait_ge(head_std, h + 1)
                dve.reciprocal(rstd[:, :], std[:, :]).then_inc(norm_step, 1)
                dve.wait_ge(norm_step, t + 9)
                for c in range(NS):
                    dve.tensor_scalar(hn[:, c, :], hn[:, c, :], mv[:, c, 0:1], rstd[:, c:c + 1], ALU.subtract,
                                      ALU.mult).then_inc(norm_step, 1)
                for c in range(NS):
                    dve.wait_ge(norm_step, t + 10 + c)
                    dve.wait_ge(o_sig, NS * (h // 2 + 1))
                    y = y_ml[:, c, h * HD:(h + 1) * HD]
                    dve.tensor_tensor(y, y, hn[:, c, :], ALU.mult).then_inc(y_ready, 1)

            def mix_work(n):
                kind = MIX[n]
                if n - 1 in LAST_QK:
                    h = LAST_QK[n - 1]
                    dve.wait_ge(decay_ready, h + 1)
                    for j in range(NS):
                        dve.wait_ge(scores_done, NS * h + j + 1)
                        s = sc[:, SC_AT[j]:SC_AT[j] + SC_W[j]]
                        dve.scalar_tensor_tensor(s, ps[:, B_S + j % 2, 0:SC_W[j]], Q_SCALE, s, ALU.mult,
                                                 ALU.mult).then_inc(p_raw, 1)
                if n == 0:
                    gates_a()
                if kind[0] == "v" and kind[2] == 3:
                    for c in range(NS):
                        dve.wait_ge(vp_hi, NS * kind[1] + c + 1)
                        dve.tensor_tensor(v_lo[:, c, :, 0:HD], ps[:, B_V + c, :].rearrange("p (h e) -> p h e", h=2),
                                          v_hi[:, c, :, 0:HD].bitcast(F32), ALU.subtract).then_inc(vp_lo, 1)
                if n == 6:
                    dve.wait_ge(gate_turned, 1)
                    dve.tensor_copy(gate_cols[:, :, :, :], ps[:, B_V, 0:32].rearrange("p (a c h) -> p a c h", a=2, c=NS)
                                    ).then_inc(gate_cols_ready, 1)
                    dve.wait_ge(gate_cols_ready, 1)
                if kind[0] == "qk":
                    dve.wait_ge(qk_h, 4 * kind[1] + kind[2] + 1)
                    dve.tensor_tensor(qk_lo[:, kind[2], :], ps[:, B_V + kind[2], :],
                                      qk_hi[:, kind[2], :].bitcast(F32), ALU.subtract).then_inc(qk_l, 1)
                h = LAST_QK.get(n)
                if h is not None:
                    dve.wait_ge(g_spread, h + 1)
                    if h:
                        dve.wait_ge(p_h, h)
                    for j in range(NS):
                        last = dve.tensor_scalar(sc[:, SC_AT[j]:SC_AT[j] + SC_W[j]], ps[:, B_S, P * j:SEQ],
                                                 gate_cols[:, 0, j, h:h + 1], 0.0, ALU.subtract, ALU.max)
                    last.then_inc(decay_arg, 1)

            def mix_work_b(n):
                h = LAST_QK.get(n)
                if n == 0:
                    gates_b()
                if n == 1:
                    doubling(0, 5, ALU.add, 6)
                if n == 2:
                    doubling(5, 9, ALU.add, 11)
                    gates_mid()
                if n == 3:
                    doubling(0, 9, ALU.max, 18)
                if n == 5:
                    dve.wait_ge(gate_dve, 27)
                    dve.tensor_tensor(g_t2, g_t2, g_x1[:, 256:768], ALU.add).then_inc(gate_dve, 1)
                    dve.wait_ge(gate_act, 3)
                    dve.sem_inc(gates_ready, 1)
                if h is not None:
                    dve.wait_ge(decay_exp, h + 1)
                    for j in range(NS):
                        d = sc[:, SC_AT[j]:SC_AT[j] + P]
                        last = dve.tensor_tensor(d, d, causal[:, :], ALU.mult)
                    last.then_inc(decay_ready, 1)
                if n - 1 in LAST_QK:
                    h = LAST_QK[n - 1]
                    dve.wait_ge(p_h, h + 1)
                    dve.tensor_tensor(p_lo[:, :], sc, p_hi[:, :].bitcast(F32), ALU.subtract).then_inc(p_l, 1)
                if n - 2 in LAST_QK:
                    norm_heads(LAST_QK[n - 2])

            def conv_work(chunk, part):
                if part == 1:
                    dve.wait_ge(tile_done, chunk * 3 + (CONV0 + 2))
                    dve.wait_ge(conv_c, chunk + 1)
                    dve.tensor_tensor(uc[:, 2:2 + SEQ], ps[:, B_V + 1, :], ux[:, :], ALU.mult).then_inc(conv_u, 1)
                    dve.wait_ge(conv_u, chunk + 1)
                    w = cw[:, chunk, :] if isinstance(chunk, int) else cw[:, bass.ds(chunk, 1), :].rearrange("p o w -> p (o w)")
                    dve.tensor_scalar(ut[:, :], uc[:, 2:2 + SEQ], w[:, 2:3], None, ALU.mult).then_inc(conv_step, 1)
                    for lag in (1, 2):
                        dve.wait_ge(conv_step, chunk * 3 + lag)
                        dve.scalar_tensor_tensor(ut[:, :], uc[:, 2 - lag:2 - lag + SEQ], w[:, 2 - lag:3 - lag], ut[:, :],
                                                 ALU.mult, ALU.add).then_inc(conv_step, 1)
                if part == 2:
                    dve.wait_ge(tile_done, chunk * 3 + (CONV0 + 3))
                    dve.wait_ge(conv_step, chunk * 3 + 3)
                    y = y_cv[:, chunk, :] if isinstance(chunk, int) else \
                        y_cv[:, bass.ds(chunk, 1), :].rearrange("p o t -> p (o t)")
                    dve.tensor_tensor(y, ps[:, B_V + 2, :], ut[:, :], ALU.mult).then_inc(conv_y, 1)

            def turn_y(m):
                dve.wait_ge(ym_h, m + 1)
                dve.scalar_tensor_tensor(ym_lo[:, m, :], ps[:, m % 4, :], gain_c[:, m:m + 1],
                                         ym_hi[:, m, :].bitcast(F32), ALU.mult, ALU.subtract).then_inc(ym_l, 1)

            dve.wait_ge(x_in[0], 16)
            for k in range(4):
                split_x(k)
            split(0, 0)
            for k in range(4, KD):
                split_x(k)
            split(1, 1)
            for n in range(CONV_LOOP0):
                if n < CONV0 or n - 1 in LAST_QK:
                    mix_work(n)
                split(n + 2, n + 2)
                mix_work_b(n)
                if n >= CONV0:
                    if n == CONV0:
                        dve.wait_ge(pads, 3)
                    conv_work(*MIX[n][1:])
                if n == CONV_LOOP0 - 2:
                    for m in range(4):
                        turn_y(m)
                if n == CONV_LOOP0 - 1:
                    for m in range(4, 8):
                        turn_y(m)
            with dve.Fori(0, CONV_TURNS) as i:
                for j in range(6):
                    split(i * 6 + (CONV_LOOP0 + j + 2), CONV_LOOP0 + j + 2)
                    conv_work(i * 2 + (CONV_PEELED + j // 3), j % 3)

            def ln_stats(c):
                for q in range(4):
                    dve.bn_stats(bstat[:, c, q, :], rows[:, c, 512 * q:512 * q + 512]).then_inc(ln_step, 1)
                dve.wait_ge(ln_step, 4 * (c + 1))
                last = dve.bn_aggr(mv[:, c, :], bstat[:, c, :, :].rearrange("p a b -> p (a b)"))
                if c % 2:
                    last.then_inc(ln_var, 1)

            def ln_norm(c):
                if c % 2 == 0:
                    dve.wait_ge(ln_std, c // 2 + 1)
                    dve.reciprocal(rstd[:, c:c + 2], std[:, c:c + 2]).then_inc(rstd_step, 1)
                    dve.wait_ge(rstd_step, c // 2 + 1)
                dve.tensor_scalar(rows[:, c, :], rows[:, c, :], mv[:, c, 0:1], rstd[:, c:c + 1], ALU.subtract,
                                  ALU.mult).then_inc(zn_ready, 1)

            for i in range(N_OUT):
                n = OUT0 + i + 2
                if i < N_OUT - 1:
                    split(n, n)
                if i < 8:
                    dve.wait_ge(yc_h, i + 1)
                    dve.tensor_tensor(act_lo[:, :, i, :], y_cv[:, i, :].rearrange("p (a t) -> p a t", a=2),
                                      act_hi[:, :, i, :].bitcast(F32), ALU.subtract).then_inc(yc_l, 1)
                if i % KD == KD - 1:
                    half = i // KD
                    dve.wait_ge(tile_done, OUT0 + i + 1)
                    dve.wait_ge(res_in[half], 16)
                    for b in range(8):
                        x = rows[:, 2 * half + b // 4, 512 * (b % 4):512 * (b % 4) + 512]
                        dve.scalar_tensor_tensor(x, x, ALPHA, ps[:, b, :], ALU.mult, ALU.add).then_inc(z_ready, 1)
                if i in (KD, KD + 1):
                    dve.wait_ge(z_ready, 8)
                    ln_stats(i - KD)
                if i in (KD + 2, KD + 3):
                    ln_norm(i - KD - 2)
            dve.wait_ge(z_ready, 16)
            ln_stats(2)
            ln_stats(3)
            ln_norm(2)
            ln_norm(3)
            for k in range(KD):
                dve.wait_ge(x1_turned, k + 1)
                if k >= 4:
                    dve.wait_ge(x1_l, k - 3)
                dve.tensor_scalar(x1_full[:, k % 4, :], ps[:, 2 + k % 6, :], ln1_c[:, 0, k:k + 1],
                                  ln1_c[:, 1, k:k + 1], ALU.mult, ALU.add).then_inc(x1_full_s, 1)

            def up_work(i, t, static):
                dst = f_gate if t % 2 else f_val
                if static:
                    c = (8 * i + t) * 4
                    pars = [fc[:, c + r:c + r + 1] for r in range(4)]
                else:
                    pars = [fc[:, bass.ds(i * 32 + (4 * t + r), 1)] for r in range(4)]
                up = i * 8 + t
                if t % 2:
                    if not static or i or t > 1:
                        dve.wait_ge(silu_done, i * 4 + t // 2)
                elif not static or i or t:
                    dve.wait_ge(prod_ready, i * 4 + t // 2)
                last = conv_terms(dve, dst, ps[:, t % 2, :], pars, ff_step, up * 2)
                last.then_inc(ff_conv, 1)

            def hidden(i, pair):
                dve.wait_ge(silu_done, i * 4 + (pair + 1))
                dve.wait_ge(ff_conv, i * 8 + (2 * pair + 1))
                if not (isinstance(i, int) and i == 0 and pair == 0):
                    dve.wait_ge(h_h, i * 4 + pair)
                dve.tensor_tensor(f_prod[:, :], f_silu[:, :], f_val[:, :], ALU.mult).then_inc(prod_ready, 1)
                dve.wait_ge(prod_ready, i * 4 + (pair + 1))
                dve.wait_ge(h_h, i * 4 + (pair + 1))
                dve.tensor_tensor(h_lo[:, pair, :], f_prod[:, :], h_hi[:, pair, :].bitcast(F32),
                                  ALU.subtract).then_inc(h_l, 1)

            def group(i, last):
                for j in range(BODY - last):
                    up = j + 1 if j < 7 else 0
                    is_up = j < (7 if last else 8)
                    if is_up:
                        dve.wait_ge(tile_done, i * BODY + (FF0 + 2 + j))
                        up_work(i if j < 7 else i + 1, up, last)
                    if not (last and j == BODY - 2):
                        split(i * BODY + (FF0 + 2 + j), j + 1)
                    if j < 7 and j % 2 == 0:
                        hidden(i, j // 2)
                    if not is_up:
                        q = j - (7 if last else 8)
                        for c in range(NS):
                            dve.wait_ge(down_done, i * 16 + (4 * q + c + 1))
                            x = rows[:, c, 512 * q:512 * q + 512]
                            dve.tensor_tensor(x, x, ps[:, B_V + c, :], ALU.add).then_inc(added, 1)
                            if last:
                                dve.wait_ge(added, i * 16 + 4 * q + c + 1)
                                dve.bn_stats(bstat[:, c, q, :], x).then_inc(ln_step, 1)

            dve.wait_ge(tile_done, FF0 + 1)
            up_work(0, 0, True)
            split(FF0 + 1, 0)
            dve.wait_ge(res_ready, NS)
            with dve.Fori(0, GROUPS - 1) as i:
                group(i, False)
            group(GROUPS - 1, True)
            dve.wait_ge(ln2_in, 32)
            for c in range(NS):
                dve.wait_ge(ln_step, 16 + 13 + c)
                dve.bn_aggr(mv[:, c, :], bstat[:, c, :, :].rearrange("p a b -> p (a b)")).then_inc(ln_var, 1)
            for c in range(NS):
                dve.wait_ge(ln_std, 3 + c)
                dve.reciprocal(rstd[:, c:c + 1], std[:, c:c + 1]).then_inc(rstd_step, 1)
                dve.wait_ge(rstd_step, 3 + c)
                dve.tensor_scalar(rows[:, c, :], rows[:, c, :], mv[:, c, 0:1], rstd[:, c:c + 1], ALU.subtract,
                                  ALU.mult).then_inc(zn_ready, 1)
                dve.wait_ge(zn_ready, NS + c + 1)
                dve.tensor_tensor(rows[:, c, :], rows[:, c, :], ln_rows[:, 0, :], ALU.mult).then_inc(gained, 1)

        @block.tensor
        def _(pe):
            def mm3(dst, a, b, first, last):
                pe.matmul(dst, a[0], b[0], start=first, stop=False)
                pe.matmul(dst, a[0], b[1], start=False, stop=False)
                return pe.matmul(dst, a[1], b[0], start=False, stop=last)

            def w_tile(s, lo, hi):
                return w_hi[:, s % SPLIT, lo:hi], w_lo[:, s % SPLIT, lo:hi]

            def acts(k):
                return act_hi[:, :, k, :], act_lo[:, :, k, :]

            def acts_block(k, c):
                at = P * (c % 2)
                return act_hi[:, c // 2, k, at:at + P], act_lo[:, c // 2, k, at:at + P]

            def bank(b):
                return ps[:, b, :].rearrange("p (a t) -> p a t", a=2)

            def by_features(n, s, b):
                pe.wait_ge(tile_lo, n + 1)
                for k in range(KD):
                    if isinstance(n, int) and n == 0:
                        pe.wait_ge(x_lo, k + 1)
                    last = mm3(bank(b), w_tile(s, P * k, P * k + P), acts(k), k == 0, k == KD - 1)
                last.then_inc(tile_done, 1)

            def by_positions(n, b, q):
                pe.wait_ge(tile_lo, n + 1)
                for kk in range(4):
                    k = 4 * q + kk
                    for c in range(NS):
                        last = mm3(ps[:, b + c, :], acts_block(k, c), w_tile(n, 512 * kk, 512 * kk + 512),
                                   k == 0, k == KD - 1)
                last.then_inc(tile_done, 1)

            def spread_g(h):
                if h == 0:
                    pe.wait_ge(o_sig, NS)
                else:
                    pe.wait_ge(head_read, NS * h)
                    pe.wait_ge(o_sig, NS * (h // 2 + 1))
                pe.matmul(ps[:, B_S, :], head_rows[:, h, :], g_x1[:, 256:768], start=True, stop=True).then_inc(g_spread, 1)

            def scores(h):
                pe.wait_ge(qk_l, 4 * (h + 1))
                pe.wait_ge(decay_arg, h + 1)
                for j in range(NS):
                    if j >= 2:
                        pe.wait_ge(p_raw, NS * h + j - 1)
                    for d in range(2):
                        at = P * j
                        last = mm3(ps[:, B_S + j % 2, 0:SC_W[j]],
                                   (qk_hi[:, 2 + d, at:at + P], qk_lo[:, 2 + d, at:at + P]),
                                   (qk_hi[:, d, at:SEQ], qk_lo[:, d, at:SEQ]), d == 0, d == 1)
                    last.then_inc(scores_done, 1)

            def values(h):
                pe.wait_ge(p_l, h + 1)
                pe.wait_ge(vp_lo, NS * (h // 2 + 1))
                if h == 0:
                    pe.wait_ge(pads, 3)
                else:
                    pe.wait_ge(head_read, NS * h)
                for c in range(NS):
                    for j in range(c + 1):
                        at = SC_AT[j] + P * (c - j)
                        last = mm3(ps[:, c, 0:HD + 2], (p_hi[:, at:at + P], p_lo[:, at:at + P]),
                                   (v_hi[:, j, h % 2, :], v_lo[:, j, h % 2, :]), j == 0, j == c)
                    last.then_inc(pv_done, 1)

            def turn_gates():
                pe.wait_ge(gates_ready, 1)
                pe.wait_ge(vp_lo, NS)
                for a, src in enumerate((g_t1, g_t2)):
                    for c in range(NS):
                        at = (a * NS + c) * HEADS
                        last = pe.transpose(ps[:, B_V, at:at + HEADS], src[:, P * c:P * c + P], ident[0:HEADS, 0:HEADS])
                last.then_inc(gate_turned, 1)

            def turn_y(m):
                pe.wait_ge(y_ready, 4 * (m // 2 + 1))
                if m < 4:
                    pe.wait_ge(head_read, NS * HEADS)
                    pe.wait_ge(p_l, HEADS)
                else:
                    pe.wait_ge(ym_l, m - 3)
                for c in range(NS):
                    last = pe.transpose(ps[:, m % 4, P * c:P * c + P], y_ml[:, c, P * m:P * m + P], ident[:, :])
                last.then_inc(y_turned, 1)

            def conv_tile(n, s, chunk, part):
                if isinstance(chunk, int) and chunk == 0:
                    pe.wait_ge(qk_l, 16)
                else:
                    pe.wait_ge((conv_c, conv_u, conv_y)[part], chunk)
                by_features(n, s, B_V + part)

            pe.wait_ge(consts_in, 16 * 8)
            for n in range(CONV_LOOP0):
                kind = MIX[n]
                if kind[0] == "gates":
                    by_features(n, n, 0)
                elif kind[0] == "v":
                    if kind[1] and kind[2] == 0:
                        pe.wait_ge(qk_l, 8 * kind[1])
                    by_positions(n, B_V, kind[2])
                elif kind[0] == "o":
                    if kind[2] == 0:
                        if kind[1] == 0:
                            pe.wait_ge(gate_dve, 2)
                        else:
                            pe.wait_ge(head_read, 2 * NS * kind[1])
                    by_positions(n, B_O, kind[2])
                elif kind[0] == "qk":
                    _, h, j = kind
                    if h % 2 == 0:
                        pe.wait_ge(vp_lo, NS * (h // 2 + 1))
                        pe.wait_ge(gate_cols_ready, 1)
                    else:
                        pe.wait_ge(qk_l, 4 * (h - 1) + j + 1)
                    by_features(n, n, B_V + j)
                else:
                    conv_tile(n, n, kind[1], kind[2])
                if n == 5:
                    turn_gates()
                if n in LAST_QK:
                    spread_g(LAST_QK[n])
                if n - 1 in LAST_QK:
                    scores(LAST_QK[n - 1])
                if n - 2 in LAST_QK:
                    values(LAST_QK[n - 2])
                if n == CONV_LOOP0 - 2:
                    for m in range(4):
                        turn_y(m)
                if n == CONV_LOOP0 - 1:
                    for m in range(4, 8):
                        turn_y(m)
            with pe.Fori(0, CONV_TURNS) as i:
                for j in range(6):
                    conv_tile(i * 6 + (CONV_LOOP0 + j), CONV_LOOP0 + j, i * 2 + (CONV_PEELED + j // 3), j % 3)

            for i in range(N_OUT):
                n, half, k = OUT0 + i, i // KD, i % KD
                pe.wait_ge(tile_lo, n + 1)
                if i == 0:
                    pe.wait_ge(conv_y, 8)
                    pe.wait_ge(ym_l, 8)
                if 8 <= i < KD:
                    pe.wait_ge(yc_l, k - 7)
                for b in range(8):
                    if i == KD:
                        pe.wait_ge(z_ready, b + 1)
                    c = 2 * half + b // 4
                    y = (ym_hi[:, k, P * c:P * c + P], ym_lo[:, k, P * c:P * c + P]) if k < 8 else acts_block(k - 8, c)
                    last = mm3(ps[:, b, :], y, w_tile(n, 512 * (b % 4), 512 * (b % 4) + 512), k == 0, k == KD - 1)
                last.then_inc(tile_done, 1)

            pe.wait_ge(zn_ready, NS)
            for k in range(KD + 6):
                if k < KD:
                    if k >= 6:
                        pe.wait_ge(x1_full_s, k - 5)
                    for c in range(NS):
                        last = pe.transpose(ps[:, 2 + k % 6, P * c:P * c + P], rows[:, c, P * k:P * k + P], ident[:, :])
                    last.then_inc(x1_turned, 1)
                if k >= 6:
                    kk = k - 6
                    if kk == 0:
                        pe.wait_ge(tile_lo, FF0 + 1)
                    pe.wait_ge(x1_l, kk + 1)
                    last = mm3(bank(0), w_tile(FF0, P * kk, P * kk + P), acts(kk), kk == 0, kk == KD - 1)
            last.then_inc(tile_done, 1)

            def group(i, last_group):
                for j in range(BODY - last_group):
                    n = i * BODY + (FF0 + 1 + j)
                    if j < (7 if last_group else 8):
                        t = (j + 1) % 8
                        if not (isinstance(i, int) and i == 0 and j == 0):
                            pe.wait_ge(ff_conv, i * 8 + j)
                        by_features(n, FF0 + 1 + j, t % 2)
                        continue
                    q = j - (7 if last_group else 8)
                    pe.wait_ge(tile_lo, n + 1)
                    if q == 0:
                        pe.wait_ge(h_l, i * 4 + 4)
                    for c in range(NS):
                        if q or last_group:
                            pe.wait_ge(added, i * 16 + (4 * (q - 1) + c + 1))
                        else:
                            pe.wait_ge(added, i * 16 + c)
                        for f in range(FCH):
                            last = mm3(ps[:, B_V + c, :], (h_hi[:, f, P * c:P * c + P], h_lo[:, f, P * c:P * c + P]),
                                       w_tile(FF0 + 1 + j, 512 * f, 512 * f + 512), f == 0, f == FCH - 1)
                        if c == NS - 1:
                            last.then_inc(down_done, 1)
                            pe.wait_ge(down_done, i * 16 + (4 * q + c + 1))
                            pe.sem_inc(tile_done, 1)
                        else:
                            last.then_inc(down_done, 1)

            with pe.Fori(0, GROUPS - 1) as i:
                group(i, False)
            group(GROUPS - 1, True)


_SHAPES = [("x_t", (KD, P, SEQ)), ("x_rows", (NS, P, D)), ("w_mix", (N_MIX, P, TW)), ("w_out", (D, D)),
           ("w_up", (2 * D_FF // P, P, TW)), ("w_down", (D_FF // P, P, TW)), ("b_gates", (HEADS, 2)),
           ("conv_w", (P, 8, 3)), ("gain", (P, 8)), ("ln1_cols", (P, 2, KD)), ("ffn_conv", (P, 2 * D_FF // P * 4)),
           ("ln1_rows", (2, D)), ("ln2_rows", (2, D)), ("ident_in", (P, P)), ("head_rows_in", (HEADS, HEADS, P)),
           ("causal_in", (P, P))]


def kernel(**inputs):
    import numpy as np
    import concourse.bacc as bacc
    from concourse.bass_utils import run_bass_kernel_spmd

    a = {k: np.asarray(v) for k, v in inputs.items()}
    f32 = np.float32

    def by_feature_tile(w):
        return w.reshape(KD, P, P).transpose(1, 0, 2).reshape(P, TW)

    def by_position_tile(w):
        return w.reshape(4, P, 512).transpose(1, 0, 2).reshape(P, TW)

    w_in = a["w_in"][0]
    at = {"b": 0, "c": W_CONV, "h": 2 * W_CONV, "q": 3 * W_CONV, "k": 3 * W_CONV + W_ML,
          "v": 3 * W_CONV + 2 * W_ML, "o": 3 * W_CONV + 3 * W_ML, "g": 3 * W_CONV + 4 * W_ML}
    mix = np.zeros((N_MIX, P, TW), f32)
    for n, kind in enumerate(MIX):
        if kind[0] == "gates":
            w = np.zeros((D, P), f32)
            w[:, 0:HEADS] = w_in[:, at["g"]:at["g"] + HEADS]
            w[:, 32:32 + HEADS] = w_in[:, at["g"] + HEADS:at["g"] + 2 * HEADS]
            mix[n] = by_feature_tile(w)
        elif kind[0] in ("v", "o"):
            c = at[kind[0]] + kind[1] * 512
            mix[n] = by_position_tile(w_in[kind[2] * 512:kind[2] * 512 + 512, c:c + 512])
        else:
            c = at["qk"[kind[2] // 2]] + kind[1] * HD + kind[2] % 2 * P if kind[0] == "qk" \
                else at["chb"[kind[2]]] + kind[1] * P
            mix[n] = by_feature_tile(w_in[:, c:c + P])
    nf = D_FF // P
    w_up = a["w_up"][0].reshape(KD, P, 2, nf, P).transpose(3, 2, 1, 0, 4).reshape(2 * nf, P, TW)
    w_down = a["w_down"][0].reshape(GROUPS, FCH, P, 4, 512).transpose(0, 3, 2, 1, 4).reshape(nf, P, TW)
    pars = np.concatenate([a["w_ffn_conv"][0], a["b_ffn_conv"]], 0)
    ffn_conv = pars.reshape(4, 2, nf, P).transpose(3, 2, 1, 0).reshape(P, 2 * nf * 4)
    head_rows = np.zeros((HEADS, HEADS, P), f32)
    for h in range(HEADS):
        head_rows[h, h] = 1.0
    arrays = {
        "x_t": a["x"][0].T.reshape(KD, P, SEQ),
        "x_rows": a["x"][0].reshape(NS, P, D),
        "w_mix": mix, "w_out": a["w_out"][0], "w_up": w_up, "w_down": w_down,
        "b_gates": a["b_gates"][0].reshape(2, HEADS).T,
        "conv_w": a["w_sc_conv"][0].reshape(3, 8, P).transpose(2, 1, 0),
        "gain": a["mh_gain"][0].reshape(8, P).T,
        "ln1_cols": np.stack([a["ln1_g"][0], a["ln1_b"][0]]).reshape(2, KD, P).transpose(2, 0, 1),
        "ffn_conv": ffn_conv,
        "ln1_rows": np.stack([a["ln1_g"][0], a["ln1_b"][0]]),
        "ln2_rows": np.stack([a["ln2_g"][0], a["ln2_b"][0]]),
        "ident_in": np.eye(P, dtype=f32),
        "head_rows_in": head_rows,
        "causal_in": np.triu(np.ones((P, P), f32)),
    }
    nc = bacc.Bacc("TRN2", target_bir_lowering=False, num_devices=1)
    args, given = [], {}
    for name, shape in _SHAPES:
        given[name] = np.ascontiguousarray(arrays[name])
        assert given[name].shape == shape, name
        args.append(nc.dram_tensor(name, shape, F32, kind="ExternalInput").ap())
    out = nc.dram_tensor("out", (SEQ, D), F32, kind="ExternalOutput").ap()
    build(nc, *args, out)
    r = run_bass_kernel_spmd(nc, [given], core_ids=[0])
    return r.results[0]["out"].reshape(1, SEQ, D)
```

```python
from contextlib import ExitStack

import concourse.bass as bass
from concourse import mybir

F32 = mybir.dt.float32
F32R = mybir.dt.float32r
ALU = mybir.AluOpType
ACT = mybir.ActivationFunctionType

P = 128
SEQ, D, W_CONV, W_ML, D_FF = 512, 2048, 1024, 1024, 5632
HEADS = 4
HD = W_ML // HEADS
TW = 2048
KD = D // P
NS = SEQ // P
ALPHA = 2.0 ** 0.25
LN_EPS, HEAD_EPS = 1e-5, 1e-6
Q_SCALE = float(HD) ** -0.5
RAW, SPLIT = 3, 2
FCH = 4
GROUPS = D_FF // P // FCH
TAIL = 1280
BODY = 3 * FCH

MIX = []
for _pair in range(HEADS // 2):
    MIX += [("v", _pair, q) for q in range(4)] + [("o", _pair, q) for q in range(4)]
    if _pair == 0:
        MIX += [("gates",)]
    MIX += [("qk", 2 * _pair + s, j) for s in range(2) for j in range(4)]
MIX += [("conv", c, j) for c in range(W_CONV // P) for j in range(3)]
N_MIX = len(MIX)
N_OUT = 2 * KD
OUT0 = N_MIX
FF0 = N_MIX + N_OUT
CONV0 = MIX.index(("conv", 0, 0))
GATES = MIX.index(("gates",))
CONV_PEELED = 2
CONV_LOOP0 = CONV0 + 3 * CONV_PEELED
CONV_TURNS = (W_CONV // P - CONV_PEELED) // 2
assert CONV_LOOP0 % RAW == 0 and FF0 % RAW == 2 and BODY % 6 == 0
LAST_QK = {MIX.index(("qk", h, 3)): h for h in range(HEADS)}
B_O, B_S, B_V, B_GATES, B_TURN = 0, 2, 4, 7, 1
X_PARTS = [(0, 1), (1, 2), (2, 4), (4, 8), (8, 12), (12, 16)]
SC_AT = [0, 512, 896, 1152]
SC_W = [SEQ - P * j for j in range(NS)]
SC_ALL = sum(SC_W)
Y_CONV = 4096
G_X0, G_X1, G_T1, G_T2 = Y_CONV, Y_CONV + 768, Y_CONV + 1536, Y_CONV + 2048
HN_AT = Y_CONV + 1792
SC_BUF = Y_CONV + 4096 - SC_ALL


def build(nc, x_t, x_rows, w_mix, w_out, w_up, w_down, b_gates, conv_w, gain, ln1_cols, ffn_conv,
          ln1_rows, ln2_rows, ident_in, head_rows_in, causal_in, out):
    ctx = ExitStack()
    with ctx:
        def sb(name, shape, dt=F32, scope=ctx):
            return scope.enter_context(nc.sbuf_tensor(name, shape, dt))

        def sem(name):
            return ctx.enter_context(nc.semaphore(name))

        raw = sb("raw", [P, RAW, TW])
        w_hi = sb("w_hi", [P, SPLIT, TW], F32R)
        w_lo = sb("w_lo", [P, SPLIT, TW], F32R)
        act_hi = sb("act_hi", [P, 2, KD, 256], F32R)
        act_lo = sb("act_lo", [P, 2, KD, 256], F32R)
        stream = sb("stream", [P, NS * D])
        ident = sb("ident", [P, P])
        causal = sb("causal", [P, P])
        head_rows = sb("head_rows", [HEADS, HEADS, P])
        bg = sb("bg", [HEADS, 2])
        cw = sb("cw", [P, 8, 3])
        gain_c = sb("gain_c", [P, 8])
        ln1_c = sb("ln1_c", [P, 2, KD])
        fc = sb("fc", [P, 2 * D_FF // P * 4])
        gate_cols = sb("gate_cols", [P, 2, NS, HEADS])
        den = sb("den", [P, 4, NS])
        bstat = sb("bstat", [P, NS, 4, 6])
        mv = sb("mv", [P, NS, 2])
        std = sb("std", [P, NS])
        rstd = sb("rstd", [P, NS])
        nbias = sb("nbias", [P, NS])
        eps = sb("eps", [P, 2])
        uc = sb("uc", [P, 2 + SEQ])
        ut = sb("ut", [P, SEQ])
        ux = sb("ux", [P, SEQ])
        with ExitStack() as stage:
            v_hi = sb("v_hi", [P, NS, 2, HD + 2], F32R, stage)
            v_lo = sb("v_lo", [P, NS, 2, HD + 2], F32R, stage)
            qk_hi = sb("qk_hi", [P, 4, SEQ], F32R, stage)
            qk_lo = sb("qk_lo", [P, 4, SEQ], F32R, stage)
            p_hi = sb("p_hi", [P, SC_ALL], F32R, stage)
            p_lo = sb("p_lo", [P, SC_ALL], F32R, stage)
        with ExitStack() as stage:
            ym_hi = sb("ym_hi", [P, 8, SEQ], F32R, stage)
            ym_lo = sb("ym_lo", [P, 8, SEQ], F32R, stage)
        with ExitStack() as stage:
            h_hi = sb("h_hi", [P, FCH, SEQ], F32R, stage)
            h_lo = sb("h_lo", [P, FCH, SEQ], F32R, stage)
            x1_full = sb("x1_full", [P, 4, SEQ], F32, stage)
            f_val, f_gate, f_silu, f_prod = (x1_full[:, j, :] for j in range(4))
            ln_rows = sb("ln_rows", [P, 2, D], F32, stage)
        ps = ctx.enter_context(nc.psum_tensor("ps", [P, 8, 512], F32))

        g_x0, g_x1 = (stream[0:HEADS, g:g + 768] for g in (G_X0, G_X1))
        g_t1, g_t2 = (stream[0:HEADS, g:g + 512] for g in (G_T1, G_T2))
        hn = stream[:, HN_AT:HN_AT + NS * HD].rearrange("p (c e) -> p c e", c=NS)
        sc = stream[:, SC_BUF:SC_BUF + SC_ALL]
        y_ml = stream[:, 0:4096].rearrange("p (c e) -> p c e", c=NS)
        y_cv = stream[:, Y_CONV:Y_CONV + 4096].rearrange("p (k t) -> p k t", k=8)
        x_raw = stream[:, :].rearrange("p (k t) -> p k t", k=KD)
        rows = stream[:, :].rearrange("p (c n) -> p c n", c=NS)

        consts_in = sem("consts_in")
        x_in = [sem(f"x_in{i}") for i in range(len(X_PARTS))]
        first_in = [sem(f"first_in{i}") for i in range(4)]
        first_hi, first_lo = sem("first_hi"), sem("first_lo")
        raw_in = [sem(f"raw_in{i}") for i in range(RAW)]
        res_in = [sem(f"res_in{i}") for i in range(2)]
        ln1_in = sem("ln1_in")
        ln2_in = sem("ln2_in")
        x_hi, x_lo = sem("x_hi"), sem("x_lo")
        tile_hi, tile_lo, tile_done = sem("tile_hi"), sem("tile_lo"), sem("tile_done")
        pads = sem("pads")
        gate_dve, gate_act = sem("gate_dve"), sem("gate_act")
        gates_ready, gate_turned, gate_cols_ready = sem("gates_ready"), sem("gate_turned"), sem("gate_cols_ready")
        vp_hi, vp_lo, o_sig = sem("vp_hi"), sem("vp_lo"), sem("o_sig")
        qk_h, qk_l = sem("qk_h"), sem("qk_l")
        g_spread, decay_arg, decay_exp, decay_ready = sem("g_spread"), sem("decay_arg"), sem("decay_exp"), sem("decay_ready")
        scores_done, p_raw, p_h, p_l = sem("scores_done"), sem("p_raw"), sem("p_h"), sem("p_l")
        pv_done, norm_step, head_read = sem("pv_done"), sem("norm_step"), sem("head_read")
        head_var, head_std, y_ready = sem("head_var"), sem("head_std"), sem("y_ready")
        y_turned, ym_h, ym_l = sem("y_turned"), sem("ym_h"), sem("ym_l")
        conv_c, conv_u, conv_step, conv_y = sem("conv_c"), sem("conv_u"), sem("conv_step"), sem("conv_y")
        yc_h, yc_l = sem("yc_h"), sem("yc_l")
        z_ready, ln_step, ln_var, ln_std, zn_ready = sem("z_ready"), sem("ln_step"), sem("ln_var"), sem("ln_std"), sem("zn_ready")
        out_first = sem("out_first")
        x1_turned, x1_full_act, x1_full_dve = sem("x1_turned"), sem("x1_full_act"), sem("x1_full_dve")
        x1_h, x1_lo_pool, x1_lo_dve = sem("x1_h"), sem("x1_lo_pool"), sem("x1_lo_dve")
        rstd_step = sem("rstd_step")
        pool_step, res_ready = sem("pool_step"), sem("res_ready")
        ff_step, ff_conv, silu_done, prod_ready = sem("ff_step"), sem("ff_conv"), sem("silu_done"), sem("prod_ready")
        h_h, h_l, down_done, down_free = sem("h_h"), sem("h_l"), sem("down_done"), sem("down_free")
        tail_bias, tail_normed, tail_step = sem("tail_bias"), sem("tail_normed"), sem("tail_step")
        gained, out_dve, out_pool, stored = sem("gained"), sem("out_dve"), sem("out_pool"), sem("stored")

        def x1_piece(m):
            return x1_full[:, m % 8 // 2, m % 2 * 256:m % 2 * 256 + 256]

        def wait_x1_lo(eng, m):
            if m < KD or m % 2 == 0:
                eng.wait_ge(x1_lo_pool, m + 1 if m < KD else KD + (m - KD) // 2 + 1)
            else:
                eng.wait_ge(x1_lo_dve, (m - KD) // 2 + 1)

        def x1_bank(m):
            return 1 + m // 2 % 3 if m < KD else 1 + (m - KD) // 2 % 7

        block = ctx.enter_context(nc.Block())

        def conv_terms(eng, dst, src, pars, step, count):
            eng.tensor_scalar(dst[:, :], src[:, :], pars[2], pars[3], ALU.mult, ALU.add).then_inc(step, 1)
            for lag in (1, 2):
                eng.wait_ge(step, count + lag)
                last = eng.scalar_tensor_tensor(dst[:, lag:SEQ], src[:, 0:SEQ - lag], pars[2 - lag],
                                                dst[:, lag:SEQ], ALU.mult, ALU.add)
                if lag == 1:
                    last.then_inc(step, 1)
            return last

        @block.sync
        def _(sp):
            def load(src, n, s):
                if not (isinstance(n, int) and n < RAW):
                    sp.wait_ge(tile_lo, n - RAW + 1)
                sp.dma_start(raw[:, s % RAW, :], src).then_inc(raw_in[s % RAW], 16)

            def load_x(i):
                a, b = X_PARTS[i]
                sp.dma_start(x_raw[:, a:b, :], x_t[a:b].rearrange("k p t -> p k t")).then_inc(x_in[i], 16)

            def load_first(q):
                sp.dma_start(raw[:, 0, 512 * q:512 * q + 512], w_mix[0][:, 512 * q:512 * q + 512]).then_inc(first_in[q], 16)

            load_first(0)
            load_x(0)
            load_x(1)
            load_first(1)
            load_x(2)
            load_first(2)
            load_first(3)
            load_x(3)
            load(w_mix[1], 1, 1)
            load_x(4)
            load(w_mix[2], 2, 2)
            load_x(5)
            for n in range(3, CONV_LOOP0):
                load(w_mix[n], n, n)
            with sp.Fori(0, CONV_TURNS) as i:
                for j in range(6):
                    load(w_mix[bass.ds(i * 6 + (CONV_LOOP0 + j), 1)].rearrange("o p n -> (o p) n"),
                         i * 6 + (CONV_LOOP0 + j), CONV_LOOP0 + j)
            for i in range(N_OUT):
                k = i % KD
                r = W_CONV + k * P if k < 8 else (k - 8) * P
                load(w_out[r:r + P, :], OUT0 + i, OUT0 + i)
            load(w_up[0], FF0, FF0)

            def group(i, last):
                for j in range(7 if last else 8):
                    src = w_up[8 * i + 1 + j] if last else w_up[bass.ds(i * 8 + (1 + j), 1)].rearrange("o p n -> (o p) n")
                    load(src, i * BODY + (FF0 + 1 + j), j)
                for j in range(4):
                    at = (7 if last else 8) + j
                    src = w_down[4 * i + j] if last else w_down[bass.ds(i * 4 + j, 1)].rearrange("o p n -> (o p) n")
                    load(src, i * BODY + (FF0 + 1 + at), at)

            with sp.Fori(0, GROUPS - 1) as i:
                group(i, False)
            group(GROUPS - 1, True)
            sp.wait_ge(res_ready, NS)
            for r in range(2):
                sp.dma_start(ln_rows[:, r, :], ln2_rows[r].partition_broadcast(P)).then_inc(ln2_in, 16)
            for c in range(NS):
                sp.wait_ge(out_dve, c + 1)
                sp.dma_start(out[c * P:(c + 1) * P, 0:TAIL], rows[:, c, 0:TAIL]).then_inc(stored, 16)
                sp.wait_ge(out_pool, c + 1)
                sp.dma_start(out[c * P:(c + 1) * P, TAIL:D], rows[:, c, TAIL:D]).then_inc(stored, 16)
            sp.wait_ge(stored, 32 * NS)

        @block.gpsimd
        def _(pool):
            pool.memset(v_hi[:, :, :, HD:HD + 2].bitcast(F32), 1.0).then_inc(pads, 1)
            pool.memset(uc[:, 0:2], 0.0).then_inc(pads, 1)
            pool.memset(v_lo[:, :, :, HD:HD + 2].bitcast(F32), 0.0).then_inc(pads, 1)
            pool.memset(eps[:, 0:1], HEAD_EPS).then_inc(pads, 1)
            pool.memset(eps[:, 1:2], LN_EPS).then_inc(pads, 1)
            for dst, src in ((ident[:, :], ident_in), (causal[:, :], causal_in), (bg[:, :], b_gates),
                             (head_rows[:, :, :], head_rows_in), (cw[:, :, :], conv_w), (gain_c[:, :], gain),
                             (ln1_c[:, :, :], ln1_cols), (fc[:, :], ffn_conv)):
                pool.dma_start(dst, src).then_inc(consts_in, 16)
            pool.wait_ge(y_turned, 8)
            pool.dma_start(rows[:, 0:2, :], x_rows[0:2].rearrange("c p n -> p c n")).then_inc(res_in[0], 16)
            pool.wait_ge(yc_l, 8)
            pool.dma_start(rows[:, 2:4, :], x_rows[2:4].rearrange("c p n -> p c n")).then_inc(res_in[1], 16)
            pool.wait_ge(tile_done, FF0)
            for r in range(2):
                pool.dma_start(ln_rows[:, r, :], ln1_rows[r].partition_broadcast(P)).then_inc(ln1_in, 16)
            for m in [*range(KD), *range(KD, 2 * KD, 2)]:
                pool.wait_ge(x1_h, m + 1)
                pool.tensor_tensor(act_lo[:, m // KD, m % KD, :], x1_piece(m), act_hi[:, m // KD, m % KD, :].bitcast(F32),
                                   ALU.subtract).then_inc(x1_lo_pool, 1)
            pool.wait_ge(ln1_in, 32)
            pool.tensor_scalar(ln_rows[:, :, :], ln_rows[:, :, :], ALPHA, None, ALU.mult).then_inc(pool_step, 1)
            pool.wait_ge(x1_turned, KD)
            pool.wait_ge(pool_step, 1)
            for c in range(NS):
                pool.tensor_tensor(rows[:, c, :], rows[:, c, :], ln_rows[:, 0, :], ALU.mult).then_inc(pool_step, 1)
                pool.wait_ge(pool_step, c + 2)
                pool.tensor_tensor(rows[:, c, :], rows[:, c, :], ln_rows[:, 1, :], ALU.add).then_inc(res_ready, 1)
            pool.wait_ge(ln2_in, 32)
            for c in range(NS):
                part = rows[:, c, TAIL:D]
                pool.wait_ge(tail_normed, c + 1)
                pool.tensor_tensor(part, part, ln_rows[:, 0, TAIL:D], ALU.mult).then_inc(tail_step, 1)
                pool.wait_ge(tail_step, c + 1)
                pool.tensor_tensor(part, part, ln_rows[:, 1, TAIL:D], ALU.add).then_inc(out_pool, 1)

        @block.scalar
        def _(act):
            def split(n, s, third):
                act.wait_ge(raw_in[s % RAW], third * 16 + (16 if s % RAW else 0))
                if not (isinstance(n, int) and n < SPLIT):
                    act.wait_ge(tile_done, n - SPLIT + 1)
                act.activation(w_hi[:, s % SPLIT, :], raw[:, s % RAW, :], ACT.Copy).then_inc(tile_hi, 1)

            def split_first(q):
                act.wait_ge(first_in[q], 16)
                act.activation(w_hi[:, 0, 512 * q:512 * q + 512], raw[:, 0, 512 * q:512 * q + 512],
                               ACT.Copy).then_inc(first_hi, 1)

            def split_x(k):
                for i, (a, b) in enumerate(X_PARTS):
                    if k == a:
                        act.wait_ge(x_in[i], 16)
                act.activation(act_hi[:, :, k, :], x_raw[:, k, :].rearrange("p (a t) -> p a t", a=2),
                               ACT.Copy).then_inc(x_hi, 1)

            def mix_work(n):
                kind = MIX[n]
                h = LAST_QK.get(n)
                if n == GATES:
                    act.wait_ge(gate_dve, 5)
                    act.activation(g_x1[:, 256:768], g_x1[:, 256:768], ACT.Exp, scale=-1.0).then_inc(gate_act, 1)
                    act.wait_ge(gate_act, 1)
                    act.activation(g_x1[:, 256:768], g_x1[:, 256:768], ACT.Ln, bias=1.0).then_inc(gate_act, 1)
                if kind[0] == "v" and kind[2] == 3:
                    act.wait_ge(tile_done, n + 1)
                    if kind[1]:
                        act.wait_ge(pv_done, 2 * NS * kind[1])
                    for c in range(NS):
                        act.activation(v_hi[:, c, :, 0:HD], ps[:, B_V + c, :].rearrange("p (h e) -> p h e", h=2),
                                       ACT.Copy).then_inc(vp_hi, 1)
                if kind[0] == "o" and kind[2] == 3:
                    act.wait_ge(tile_done, n + 1)
                    for c in range(NS):
                        act.activation(y_ml[:, c, kind[1] * 512:kind[1] * 512 + 512], ps[:, B_O + c, :],
                                       ACT.Sigmoid).then_inc(o_sig, 1)
                if kind[0] == "qk":
                    act.wait_ge(tile_done, n + 1)
                    act.wait_ge(scores_done, NS * kind[1]) if kind[1] else None
                    act.activation(qk_hi[:, kind[2], :], ps[:, B_V + kind[2], :], ACT.Copy).then_inc(qk_h, 1)
                if n == GATES + 3:
                    act.wait_ge(gate_dve, 28)
                    act.activation(g_t2, g_t2, ACT.Exp, scale=-1.0).then_inc(gate_act, 1)
                if h is not None:
                    act.wait_ge(decay_arg, h + 1)
                    act.activation(sc, sc, ACT.Exp, scale=-1.0).then_inc(decay_exp, 1)
                if n - 1 in LAST_QK:
                    h = LAST_QK[n - 1]
                    act.wait_ge(p_raw, NS * (h + 1))
                    if h:
                        act.wait_ge(pv_done, NS * h)
                    act.activation(p_hi[:, :], sc, ACT.Copy).then_inc(p_h, 1)
                if n - 2 in LAST_QK:
                    act.wait_ge(head_var, LAST_QK[n - 2] + 1)
                    act.activation(std[:, :], mv[:, :, 1], ACT.Sqrt, bias=eps[:, 0:1]).then_inc(head_std, 1)

            def conv_work(chunk, part):
                if part == 0:
                    act.wait_ge(tile_done, chunk * 3 + (CONV0 + 1))
                    if not isinstance(chunk, int) or chunk > 0:
                        act.wait_ge(conv_u, chunk)
                    act.activation(ux[:, :], ps[:, B_V, :], ACT.Copy).then_inc(conv_c, 1)

            def turn_y(m):
                act.wait_ge(y_turned, m + 1)
                act.activation(ym_hi[:, m, :], ps[:, m % 4, :], ACT.Copy, scale=gain_c[:, m:m + 1]).then_inc(ym_h, 1)

            act.wait_ge(pads, 5)
            act.activation(std[:, 0:1], eps[:, 0:1], ACT.Copy)
            split_first(0)
            split_x(0)
            split_x(1)
            split_first(1)
            split_x(2)
            split_x(3)
            split_first(2)
            split_first(3)
            act.wait_ge(first_hi, 4)
            act.sem_inc(tile_hi, 1)
            for k in range(4, 8):
                split_x(k)
            split(1, 1, 0)
            act.wait_ge(consts_in, 16 * 8)
            for n in range(CONV_LOOP0):
                if n < 2:
                    for k in range(8 + 4 * n, 12 + 4 * n):
                        split_x(k)
                split(n + 2, n + 2, (n + 2) // 3)
                if n >= CONV0:
                    if n - 1 in LAST_QK or n - 2 in LAST_QK:
                        mix_work(n)
                    conv_work(*MIX[n][1:])
                else:
                    mix_work(n)
                if n == CONV_LOOP0 - 2:
                    for m in range(4):
                        turn_y(m)
                if n == CONV_LOOP0 - 1:
                    for m in range(4, 8):
                        turn_y(m)
            with act.Fori(0, CONV_TURNS) as i:
                for j in range(6):
                    split(i * 6 + (CONV_LOOP0 + j + 2), CONV_LOOP0 + j + 2, i * 2 + (CONV_LOOP0 + j + 2) // 3)
                    conv_work(i * 2 + (CONV_PEELED + j // 3), j % 3)
            def ln_sqrt(done, first, last):
                act.wait_ge(ln_var, done)
                act.activation(std[:, first:last], mv[:, first:last, 1], ACT.Sqrt, bias=eps[:, 1:2]).then_inc(ln_std, 1)

            for i in range(N_OUT - 1):
                n = OUT0 + i + 2
                split(n, n, n // 3)
                if i == KD + 1:
                    ln_sqrt(1, 0, 2)
                if i < 8:
                    act.wait_ge(tile_done, OUT0)
                    act.wait_ge(conv_y, 8)
                    act.activation(act_hi[:, :, i, :], y_cv[:, i, :].rearrange("p (a t) -> p a t", a=2),
                                   ACT.Copy).then_inc(yc_h, 1)
            def x1_full_piece(m):
                act.wait_ge(x1_turned, m // 2 + 1)
                if m >= 8:
                    wait_x1_lo(act, m - 8)
                act.activation(x1_piece(m), ps[:, x1_bank(m), m % 2 * 256:m % 2 * 256 + 256], ACT.Identity,
                               bias=ln1_c[:, 1, m:m + 1], scale=ln1_c[:, 0, m:m + 1]).then_inc(x1_full_act, 1)

            def x1_hi_piece(m):
                if m < KD:
                    act.wait_ge(x1_full_act, m + 1)
                else:
                    act.wait_ge(x1_full_dve, m - KD + 1)
                act.activation(act_hi[:, m // KD, m % KD, :], x1_piece(m), ACT.Copy).then_inc(x1_h, 1)

            for m in range(KD + 1):
                if m < KD:
                    x1_full_piece(m)
                if m:
                    x1_hi_piece(m - 1)
                if m == 10:
                    ln_sqrt(2, 2, 4)
            split(FF0 + 1, FF0 + 1, (FF0 + 1) // 3)
            for m in range(KD, 2 * KD):
                x1_hi_piece(m)

            def hidden(i, pair):
                act.wait_ge(ff_conv, i * 8 + (2 * pair + 2))
                act.activation(f_silu[:, :], f_gate[:, :], ACT.Silu).then_inc(silu_done, 1)
                act.wait_ge(prod_ready, i * 4 + (pair + 1))
                act.activation(h_hi[:, pair, :], f_prod[:, :], ACT.Copy).then_inc(h_h, 1)

            def group(i, last):
                for j in range(BODY - last):
                    if not (last and j >= BODY - 3):
                        s = j + 2
                        split(i * BODY + (FF0 + 1 + s), s, i * 4 + (FF0 + 1 + s) // 3)
                    if j < 7 and j % 2 == 0:
                        hidden(i, j // 2)
            split(FF0 + 2, FF0 + 2, (FF0 + 2) // 3)
            with act.Fori(0, GROUPS - 1) as i:
                group(i, False)
            group(GROUPS - 1, True)
            for c in range(NS + 1):
                if c < NS:
                    ln_sqrt(3 + c, c, c + 1)
                if c:
                    act.wait_ge(tail_bias, c)
                    act.activation(rows[:, c - 1, TAIL:D], rows[:, c - 1, TAIL:D], ACT.Identity,
                                   bias=nbias[:, c - 1:c], scale=rstd[:, c - 1:c]).then_inc(tail_normed, 1)

        @block.vector
        def _(dve):
            def split(n, s):
                dve.wait_ge(tile_hi, n + 1)
                dve.tensor_tensor(w_lo[:, s % SPLIT, :], raw[:, s % RAW, :], w_hi[:, s % SPLIT, :].bitcast(F32),
                                  ALU.subtract).then_inc(tile_lo, 1)

            def split_first(q):
                dve.wait_ge(first_hi, q + 1)
                at = slice(512 * q, 512 * q + 512)
                dve.tensor_tensor(w_lo[:, 0, at], raw[:, 0, at], w_hi[:, 0, at].bitcast(F32), ALU.subtract).then_inc(first_lo, 1)

            def split_x(k):
                dve.wait_ge(x_hi, k + 1)
                dve.tensor_tensor(act_lo[:, :, k, :], x_raw[:, k, :].rearrange("p (a t) -> p a t", a=2),
                                  act_hi[:, :, k, :].bitcast(F32), ALU.subtract).then_inc(x_lo, 1)

            def doubling(first, last, op, count):
                for s in range(first, last):
                    src, dst = (g_x0, g_x1) if s % 2 == 0 else (g_x1, g_x0)
                    dve.wait_ge(gate_dve, count + s - first)
                    dve.tensor_tensor(dst[:, 256:768], src[:, 256:768], src[:, 256 - 2 ** s:768 - 2 ** s],
                                      op).then_inc(gate_dve, 1)

            def gates_a():
                dve.wait_ge(consts_in, 16 * 8)
                dve.wait_ge(tile_done, GATES + 1)
                dve.tensor_scalar(g_t1, ps[0:HEADS, B_GATES, :], bg[:, 0:1], None, ALU.add).then_inc(gate_dve, 1)
                dve.tensor_copy(g_t2, ps[32:32 + HEADS, B_GATES, :]).then_inc(gate_dve, 1)
                dve.memset(g_x0[:, 0:256], 0.0)
                dve.memset(g_x1[:, 0:256], 0.0).then_inc(gate_dve, 1)
                dve.wait_ge(gate_dve, 2)
                dve.tensor_scalar(g_t2, g_t2, bg[:, 1:2], None, ALU.add).then_inc(gate_dve, 1)
                dve.wait_ge(gate_dve, 4)
                dve.scalar_tensor_tensor(g_x1[:, 256:768], g_t2, -1.0, g_t2, ALU.mult, ALU.max).then_inc(gate_dve, 1)

            def gates_b():
                dve.wait_ge(gate_act, 2)
                dve.scalar_tensor_tensor(g_x0[:, 256:768], g_t2, 0.0, g_x1[:, 256:768], ALU.min,
                                         ALU.subtract).then_inc(gate_dve, 1)

            def gates_mid():
                dve.wait_ge(gate_dve, 15)
                dve.tensor_tensor(g_t1, g_t1, g_x1[:, 256:768], ALU.subtract).then_inc(gate_dve, 1)
                dve.tensor_copy(g_t2, g_x1[:, 256:768]).then_inc(gate_dve, 1)
                dve.wait_ge(gate_dve, 16)
                dve.tensor_copy(g_x0[:, 256:768], g_t1).then_inc(gate_dve, 1)

            def norm_heads(h):
                t = h * 13
                dve.wait_ge(pv_done, NS * (h + 1))
                dve.tensor_copy(den[:, 0, :], ps[:, 0:NS, HD]).then_inc(norm_step, 1)
                dve.wait_ge(norm_step, t + 1)
                dve.scalar_tensor_tensor(den[:, 1, :], den[:, 0, :], -1.0, den[:, 0, :], ALU.mult,
                                         ALU.max).then_inc(norm_step, 1)
                dve.wait_ge(norm_step, t + 2)
                dve.tensor_tensor(den[:, 2, :], den[:, 1, :], gate_cols[:, 1, :, h], ALU.max).then_inc(norm_step, 1)
                dve.wait_ge(norm_step, t + 3)
                dve.reciprocal(den[:, 3, :], den[:, 2, :]).then_inc(norm_step, 1)
                dve.wait_ge(norm_step, t + 4)
                for c in range(NS):
                    dve.tensor_scalar(hn[:, c, :], ps[:, c, 0:HD], den[:, 3, c:c + 1], None,
                                      ALU.mult).then_inc(head_read, 1)
                for c in range(NS):
                    dve.wait_ge(head_read, NS * h + c + 1)
                    dve.bn_stats(bstat[:, c, 0, :], hn[:, c, :]).then_inc(norm_step, 1)
                for c in range(NS):
                    dve.wait_ge(norm_step, t + 5 + c)
                    last = dve.bn_aggr(mv[:, c, :], bstat[:, c, 0, :])
                last.then_inc(head_var, 1)
                dve.wait_ge(head_std, h + 1)
                dve.reciprocal(rstd[:, :], std[:, :]).then_inc(norm_step, 1)
                dve.wait_ge(norm_step, t + 9)
                for c in range(NS):
                    dve.tensor_scalar(hn[:, c, :], hn[:, c, :], mv[:, c, 0:1], rstd[:, c:c + 1], ALU.subtract,
                                      ALU.mult).then_inc(norm_step, 1)
                for c in range(NS):
                    dve.wait_ge(norm_step, t + 10 + c)
                    dve.wait_ge(o_sig, NS * (h // 2 + 1))
                    y = y_ml[:, c, h * HD:(h + 1) * HD]
                    dve.tensor_tensor(y, y, hn[:, c, :], ALU.mult).then_inc(y_ready, 1)

            def mix_work(n):
                kind = MIX[n]
                if n - 1 in LAST_QK:
                    h = LAST_QK[n - 1]
                    dve.wait_ge(decay_ready, h + 1)
                    for j in range(NS):
                        dve.wait_ge(scores_done, NS * h + j + 1)
                        s = sc[:, SC_AT[j]:SC_AT[j] + SC_W[j]]
                        dve.scalar_tensor_tensor(s, ps[:, B_S + j % 2, 0:SC_W[j]], Q_SCALE, s, ALU.mult,
                                                 ALU.mult).then_inc(p_raw, 1)
                if n == GATES:
                    gates_a()
                if kind[0] == "v" and kind[2] == 3:
                    for c in range(NS):
                        dve.wait_ge(vp_hi, NS * kind[1] + c + 1)
                        dve.tensor_tensor(v_lo[:, c, :, 0:HD], ps[:, B_V + c, :].rearrange("p (h e) -> p h e", h=2),
                                          v_hi[:, c, :, 0:HD].bitcast(F32), ALU.subtract).then_inc(vp_lo, 1)
                if n == GATES + 4:
                    dve.wait_ge(gate_turned, 1)
                    dve.tensor_copy(gate_cols[:, :, :, :], ps[:, B_TURN, 0:32].rearrange("p (a c h) -> p a c h", a=2, c=NS)
                                    ).then_inc(gate_cols_ready, 1)
                    dve.wait_ge(gate_cols_ready, 1)
                if kind[0] == "qk":
                    dve.wait_ge(qk_h, 4 * kind[1] + kind[2] + 1)
                    dve.tensor_tensor(qk_lo[:, kind[2], :], ps[:, B_V + kind[2], :],
                                      qk_hi[:, kind[2], :].bitcast(F32), ALU.subtract).then_inc(qk_l, 1)
                h = LAST_QK.get(n)
                if h is not None:
                    dve.wait_ge(g_spread, h + 1)
                    if h:
                        dve.wait_ge(p_h, h)
                    for j in range(NS):
                        last = dve.tensor_scalar(sc[:, SC_AT[j]:SC_AT[j] + SC_W[j]], ps[:, B_S, P * j:SEQ],
                                                 gate_cols[:, 0, j, h:h + 1], 0.0, ALU.subtract, ALU.max)
                    last.then_inc(decay_arg, 1)

            def mix_work_b(n):
                h = LAST_QK.get(n)
                if n == GATES:
                    gates_b()
                if n == GATES + 1:
                    doubling(0, 9, ALU.add, 6)
                    gates_mid()
                if n == GATES + 2:
                    doubling(0, 9, ALU.max, 18)
                if n == GATES + 3:
                    dve.wait_ge(gate_dve, 27)
                    dve.tensor_tensor(g_t2, g_t2, g_x1[:, 256:768], ALU.add).then_inc(gate_dve, 1)
                    dve.wait_ge(gate_act, 3)
                    dve.sem_inc(gates_ready, 1)
                if h is not None:
                    dve.wait_ge(decay_exp, h + 1)
                    for j in range(NS):
                        d = sc[:, SC_AT[j]:SC_AT[j] + P]
                        last = dve.tensor_tensor(d, d, causal[:, :], ALU.mult)
                    last.then_inc(decay_ready, 1)
                if n - 1 in LAST_QK:
                    h = LAST_QK[n - 1]
                    dve.wait_ge(p_h, h + 1)
                    dve.tensor_tensor(p_lo[:, :], sc, p_hi[:, :].bitcast(F32), ALU.subtract).then_inc(p_l, 1)
                if n - 2 in LAST_QK:
                    norm_heads(LAST_QK[n - 2])

            def conv_work(chunk, part):
                if part == 1:
                    dve.wait_ge(tile_done, chunk * 3 + (CONV0 + 2))
                    dve.wait_ge(conv_c, chunk + 1)
                    dve.tensor_tensor(uc[:, 2:2 + SEQ], ps[:, B_V + 1, :], ux[:, :], ALU.mult).then_inc(conv_u, 1)
                    dve.wait_ge(conv_u, chunk + 1)
                    w = cw[:, chunk, :] if isinstance(chunk, int) else cw[:, bass.ds(chunk, 1), :].rearrange("p o w -> p (o w)")
                    dve.tensor_scalar(ut[:, :], uc[:, 2:2 + SEQ], w[:, 2:3], None, ALU.mult).then_inc(conv_step, 1)
                    for lag in (1, 2):
                        dve.wait_ge(conv_step, chunk * 3 + lag)
                        dve.scalar_tensor_tensor(ut[:, :], uc[:, 2 - lag:2 - lag + SEQ], w[:, 2 - lag:3 - lag], ut[:, :],
                                                 ALU.mult, ALU.add).then_inc(conv_step, 1)
                if part == 2:
                    dve.wait_ge(tile_done, chunk * 3 + (CONV0 + 3))
                    dve.wait_ge(conv_step, chunk * 3 + 3)
                    y = y_cv[:, chunk, :] if isinstance(chunk, int) else \
                        y_cv[:, bass.ds(chunk, 1), :].rearrange("p o t -> p (o t)")
                    dve.tensor_tensor(y, ps[:, B_V + 2, :], ut[:, :], ALU.mult).then_inc(conv_y, 1)

            def turn_y(m):
                dve.wait_ge(ym_h, m + 1)
                dve.scalar_tensor_tensor(ym_lo[:, m, :], ps[:, m % 4, :], gain_c[:, m:m + 1],
                                         ym_hi[:, m, :].bitcast(F32), ALU.mult, ALU.subtract).then_inc(ym_l, 1)

            split_first(0)
            split_x(0)
            split_x(1)
            split_first(1)
            split_x(2)
            split_x(3)
            split_first(2)
            split_first(3)
            dve.wait_ge(first_lo, 4)
            dve.sem_inc(tile_lo, 1)
            for k in range(4, 8):
                split_x(k)
            split(1, 1)
            for n in range(CONV_LOOP0):
                if n < 2:
                    for k in range(8 + 4 * n, 12 + 4 * n):
                        split_x(k)
                if n < CONV0 or n - 1 in LAST_QK:
                    mix_work(n)
                split(n + 2, n + 2)
                mix_work_b(n)
                if n >= CONV0:
                    if n == CONV0:
                        dve.wait_ge(pads, 3)
                    conv_work(*MIX[n][1:])
                if n == CONV_LOOP0 - 2:
                    for m in range(4):
                        turn_y(m)
                if n == CONV_LOOP0 - 1:
                    for m in range(4, 8):
                        turn_y(m)
            with dve.Fori(0, CONV_TURNS) as i:
                for j in range(6):
                    if j % 3 == 1:
                        split(i * 6 + (CONV_LOOP0 + j + 2), CONV_LOOP0 + j + 2)
                    conv_work(i * 2 + (CONV_PEELED + j // 3), j % 3)
                    if j % 3 != 1:
                        split(i * 6 + (CONV_LOOP0 + j + 2), CONV_LOOP0 + j + 2)

            def ln_stats(c):
                for q in range(4):
                    dve.bn_stats(bstat[:, c, q, :], rows[:, c, 512 * q:512 * q + 512]).then_inc(ln_step, 1)
                dve.wait_ge(ln_step, 4 * (c + 1))
                last = dve.bn_aggr(mv[:, c, :], bstat[:, c, :, :].rearrange("p a b -> p (a b)"))
                if c % 2:
                    last.then_inc(ln_var, 1)

            def ln_norm(c):
                if c % 2 == 0:
                    dve.wait_ge(ln_std, c // 2 + 1)
                    dve.reciprocal(rstd[:, c:c + 2], std[:, c:c + 2]).then_inc(rstd_step, 1)
                    dve.wait_ge(rstd_step, c // 2 + 1)
                dve.tensor_scalar(rows[:, c, :], rows[:, c, :], mv[:, c, 0:1], rstd[:, c:c + 1], ALU.subtract,
                                  ALU.mult).then_inc(zn_ready, 1)

            for i in range(N_OUT):
                n = OUT0 + i + 2
                if i < N_OUT - 1 and i != KD - 1:
                    split(n, n)
                if i < 8:
                    dve.wait_ge(yc_h, i + 1)
                    dve.tensor_tensor(act_lo[:, :, i, :], y_cv[:, i, :].rearrange("p (a t) -> p a t", a=2),
                                      act_hi[:, :, i, :].bitcast(F32), ALU.subtract).then_inc(yc_l, 1)
                if i % KD == KD - 1:
                    half = i // KD
                    dve.wait_ge(res_in[half], 16)
                    for b in range(8):
                        if b == 0 and half:
                            dve.wait_ge(out_first, 1)
                        if b == 4 * half:
                            dve.wait_ge(tile_done, OUT0 + i + 1)
                        if b == 4 and half:
                            dve.wait_ge(z_ready, 12)
                            ln_stats(2)
                        x = rows[:, 2 * half + b // 4, 512 * (b % 4):512 * (b % 4) + 512]
                        dve.scalar_tensor_tensor(x, x, ALPHA, ps[:, b, :], ALU.mult, ALU.add).then_inc(z_ready, 1)
                        if b == 3 and half == 0:
                            split(n, n)
                if i in (KD, KD + 1):
                    dve.wait_ge(z_ready, 8)
                    ln_stats(i - KD)
                if i in (KD + 2, KD + 3):
                    ln_norm(i - KD - 2)
            dve.wait_ge(z_ready, 16)
            ln_stats(3)
            ln_norm(2)
            ln_norm(3)
            for k in range(KD + 2):
                m = KD + k
                if k < KD:
                    dve.wait_ge(x1_turned, m // 2 + 1)
                    wait_x1_lo(dve, m - 8)
                    dve.tensor_scalar(x1_piece(m), ps[:, x1_bank(m), m % 2 * 256:m % 2 * 256 + 256], ln1_c[:, 0, k:k + 1],
                                      ln1_c[:, 1, k:k + 1], ALU.mult, ALU.add).then_inc(x1_full_dve, 1)
                if k >= 2 and k % 2:
                    dve.wait_ge(x1_h, m - 1)
                    dve.tensor_tensor(act_lo[:, 1, k - 2, :], x1_piece(m - 2), act_hi[:, 1, k - 2, :].bitcast(F32),
                                      ALU.subtract).then_inc(x1_lo_dve, 1)
                if k == 8:
                    split(FF0 + 1, FF0 + 1)

            def up_work(i, t, static):
                dst = f_gate if t % 2 else f_val
                if static:
                    c = (8 * i + t) * 4
                    pars = [fc[:, c + r:c + r + 1] for r in range(4)]
                else:
                    pars = [fc[:, bass.ds(i * 32 + (4 * t + r), 1)] for r in range(4)]
                up = i * 8 + t
                if t % 2:
                    if not static or i or t > 1:
                        dve.wait_ge(silu_done, i * 4 + t // 2)
                elif not static or i or t:
                    dve.wait_ge(prod_ready, i * 4 + t // 2)
                last = conv_terms(dve, dst, ps[:, t % 2, :], pars, ff_step, up * 2)
                last.then_inc(ff_conv, 1)

            def hidden(i, pair):
                dve.wait_ge(silu_done, i * 4 + (pair + 1))
                dve.wait_ge(ff_conv, i * 8 + (2 * pair + 1))
                if not (isinstance(i, int) and i == 0 and pair == 0):
                    dve.wait_ge(h_h, i * 4 + pair)
                dve.tensor_tensor(f_prod[:, :], f_silu[:, :], f_val[:, :], ALU.mult).then_inc(prod_ready, 1)
                dve.wait_ge(prod_ready, i * 4 + (pair + 1))
                dve.wait_ge(h_h, i * 4 + (pair + 1))
                dve.tensor_tensor(h_lo[:, pair, :], f_prod[:, :], h_hi[:, pair, :].bitcast(F32),
                                  ALU.subtract).then_inc(h_l, 1)

            def finish(c):
                part = rows[:, c, 0:TAIL]
                dve.wait_ge(ln_std, 3 + c)
                dve.reciprocal(rstd[:, c:c + 1], std[:, c:c + 1]).then_inc(rstd_step, 1)
                dve.wait_ge(rstd_step, 3 + c)
                dve.scalar_tensor_tensor(nbias[:, c:c + 1], mv[:, c, 0:1], -1.0, rstd[:, c:c + 1], ALU.mult,
                                         ALU.mult).then_inc(tail_bias, 1)
                dve.wait_ge(ln2_in, 32)
                dve.scalar_tensor_tensor(part, part, mv[:, c, 0:1], ln_rows[:, 0, 0:TAIL], ALU.subtract,
                                         ALU.mult).then_inc(gained, 1)
                dve.wait_ge(gained, c + 1)
                dve.scalar_tensor_tensor(part, part, rstd[:, c:c + 1], ln_rows[:, 1, 0:TAIL], ALU.mult,
                                         ALU.add).then_inc(out_dve, 1)

            def group(i, last):
                for j in range(BODY - last):
                    up = j + 1 if j < 7 else 0
                    is_up = j < (7 if last else 8)
                    if is_up:
                        dve.wait_ge(tile_done, i * BODY + (FF0 + 2 + j))
                        up_work(i if j < 7 else i + 1, up, last)
                    if is_up and not (last and j >= BODY - 3):
                        split(i * BODY + (FF0 + 3 + j), j + 2)
                    if j < 7 and j % 2 == 0:
                        hidden(i, j // 2)
                    if not is_up:
                        q = j - (7 if last else 8)
                        if q == 0:
                            dve.wait_ge(res_ready, NS)
                        for c in range(NS):
                            if c < NS - 1:
                                dve.wait_ge(down_done, i * 12 + (3 * q + c + 1))
                            else:
                                dve.wait_ge(tile_done, i * BODY + (FF0 + 2 + j))
                            x = rows[:, c, 512 * q:512 * q + 512]
                            dve.tensor_tensor(x, x, ps[:, B_V + c, :], ALU.add).then_inc(down_free, 1)
                            if last:
                                dve.wait_ge(down_free, i * 16 + NS + 4 * q + c + 1)
                                dve.bn_stats(bstat[:, c, q, :], x).then_inc(ln_step, 1)
                            if last and q == 3:
                                dve.wait_ge(ln_step, 16 + 13 + c)
                                dve.bn_aggr(mv[:, c, :], bstat[:, c, :, :].rearrange("p a b -> p (a b)")).then_inc(ln_var, 1)
                                if c:
                                    finish(c - 1)
                        if not (last and j >= BODY - 3):
                            split(i * BODY + (FF0 + 3 + j), j + 2)

            dve.sem_inc(down_free, NS)
            dve.wait_ge(tile_done, FF0 + 1)
            up_work(0, 0, True)
            split(FF0 + 2, FF0 + 2)
            with dve.Fori(0, GROUPS - 1) as i:
                group(i, False)
            group(GROUPS - 1, True)
            finish(NS - 1)

        @block.tensor
        def _(pe):
            def mm3(dst, a, b, first, last):
                pe.matmul(dst, a[0], b[0], start=first, stop=False)
                pe.matmul(dst, a[0], b[1], start=False, stop=False)
                return pe.matmul(dst, a[1], b[0], start=False, stop=last)

            def w_tile(s, lo, hi):
                return w_hi[:, s % SPLIT, lo:hi], w_lo[:, s % SPLIT, lo:hi]

            def acts(k):
                return act_hi[:, :, k, :], act_lo[:, :, k, :]

            def acts_block(k, c):
                at = P * (c % 2)
                return act_hi[:, c // 2, k, at:at + P], act_lo[:, c // 2, k, at:at + P]

            def bank(b):
                return ps[:, b, :].rearrange("p (a t) -> p a t", a=2)

            def by_features(n, s, b):
                pe.wait_ge(tile_lo, n + 1)
                for k in range(KD):
                    last = mm3(bank(b), w_tile(s, P * k, P * k + P), acts(k), k == 0, k == KD - 1)
                last.then_inc(tile_done, 1)

            def by_positions(n, b, q, left=None):
                if n:
                    pe.wait_ge(tile_lo, n + 1)
                for kk in range(4):
                    k = 4 * q + kk
                    if n == 0:
                        pe.wait_ge(first_lo, kk + 1)
                    if n < 4:
                        pe.wait_ge(x_lo, k + 1)
                    for c in range(NS):
                        if left and k == 0:
                            pe.wait_ge(left[0], left[1] + c)
                        last = mm3(ps[:, b + c, :], acts_block(k, c), w_tile(n, 512 * kk, 512 * kk + 512),
                                   k == 0, k == KD - 1)
                last.then_inc(tile_done, 1)

            def spread_g(h):
                if h == 0:
                    pe.wait_ge(o_sig, NS)
                else:
                    pe.wait_ge(head_read, NS * h)
                    pe.wait_ge(o_sig, NS * (h // 2 + 1))
                pe.matmul(ps[:, B_S, :], head_rows[:, h, :], g_x1[:, 256:768], start=True, stop=True).then_inc(g_spread, 1)

            def scores(h):
                pe.wait_ge(qk_l, 4 * (h + 1))
                pe.wait_ge(decay_arg, h + 1)
                for j in range(NS):
                    if j >= 2:
                        pe.wait_ge(p_raw, NS * h + j - 1)
                    for d in range(2):
                        at = P * j
                        last = mm3(ps[:, B_S + j % 2, 0:SC_W[j]],
                                   (qk_hi[:, 2 + d, at:at + P], qk_lo[:, 2 + d, at:at + P]),
                                   (qk_hi[:, d, at:SEQ], qk_lo[:, d, at:SEQ]), d == 0, d == 1)
                    last.then_inc(scores_done, 1)

            def values(h):
                pe.wait_ge(p_l, h + 1)
                pe.wait_ge(vp_lo, NS * (h // 2 + 1))
                if h == 0:
                    pe.wait_ge(pads, 3)
                else:
                    pe.wait_ge(head_read, NS * h)
                for c in range(NS):
                    for j in range(c + 1):
                        at = SC_AT[j] + P * (c - j)
                        last = mm3(ps[:, c, 0:HD + 2], (p_hi[:, at:at + P], p_lo[:, at:at + P]),
                                   (v_hi[:, j, h % 2, :], v_lo[:, j, h % 2, :]), j == 0, j == c)
                    last.then_inc(pv_done, 1)

            def turn_gates():
                pe.wait_ge(consts_in, 16 * 8)
                pe.wait_ge(gates_ready, 1)
                pe.wait_ge(o_sig, NS)
                for a, src in enumerate((g_t1, g_t2)):
                    for c in range(NS):
                        at = (a * NS + c) * HEADS
                        last = pe.transpose(ps[:, B_TURN, at:at + HEADS], src[:, P * c:P * c + P], ident[0:HEADS, 0:HEADS])
                last.then_inc(gate_turned, 1)

            def turn_y(m):
                pe.wait_ge(y_ready, 4 * (m // 2 + 1))
                if m < 4:
                    pe.wait_ge(head_read, NS * HEADS)
                    pe.wait_ge(p_l, HEADS)
                else:
                    pe.wait_ge(ym_l, m - 3)
                for c in range(NS):
                    last = pe.transpose(ps[:, m % 4, P * c:P * c + P], y_ml[:, c, P * m:P * m + P], ident[:, :])
                last.then_inc(y_turned, 1)

            def conv_tile(n, s, chunk, part):
                if isinstance(chunk, int) and chunk == 0:
                    pe.wait_ge(qk_l, 13 + part)
                else:
                    pe.wait_ge((conv_c, conv_u, conv_y)[part], chunk)
                by_features(n, s, B_V + part)

            for n in range(CONV_LOOP0):
                kind = MIX[n]
                if kind[0] == "gates":
                    pe.wait_ge(vp_lo, NS)
                    by_features(n, n, B_GATES)
                elif kind[0] == "v":
                    by_positions(n, B_V, kind[2], (qk_l, 8 * kind[1] - 3) if kind[1] else None)
                elif kind[0] == "o":
                    if kind[2] == 0 and kind[1]:
                        pe.wait_ge(head_read, 2 * NS * kind[1])
                    by_positions(n, B_O, kind[2])
                elif kind[0] == "qk":
                    _, h, j = kind
                    if h % 2 == 0:
                        pe.wait_ge(vp_lo, NS * (h // 2 + 1))
                        if B_V + j == B_GATES:
                            pe.wait_ge(gate_dve, 2)
                    else:
                        pe.wait_ge(qk_l, 4 * (h - 1) + j + 1)
                    by_features(n, n, B_V + j)
                else:
                    conv_tile(n, n, kind[1], kind[2])
                if n == GATES + 4:
                    turn_gates()
                if n in LAST_QK:
                    spread_g(LAST_QK[n])
                if n - 1 in LAST_QK:
                    scores(LAST_QK[n - 1])
                if n - 2 in LAST_QK:
                    values(LAST_QK[n - 2])
                if n == CONV_LOOP0 - 2:
                    for m in range(4):
                        turn_y(m)
                if n == CONV_LOOP0 - 1:
                    for m in range(4, 8):
                        turn_y(m)
            with pe.Fori(0, CONV_TURNS) as i:
                for j in range(6):
                    conv_tile(i * 6 + (CONV_LOOP0 + j), CONV_LOOP0 + j, i * 2 + (CONV_PEELED + j // 3), j % 3)

            for i in range(N_OUT):
                n, half, k = OUT0 + i, i // KD, i % KD
                pe.wait_ge(tile_lo, n + 1)
                if i == 0:
                    pe.wait_ge(ym_l, 8)
                if 8 <= i < KD:
                    pe.wait_ge(yc_l, k - 7)
                for b in range(8):
                    if i == KD:
                        pe.wait_ge(z_ready, b + 1)
                    if i == 0 and 0 <= b - B_V < 3:
                        pe.wait_ge((conv_c, conv_u, conv_y)[b - B_V], 8)
                    c = 2 * half + b // 4
                    y = (ym_hi[:, k, P * c:P * c + P], ym_lo[:, k, P * c:P * c + P]) if k < 8 else acts_block(k - 8, c)
                    last = mm3(ps[:, b, :], y, w_tile(n, 512 * (b % 4), 512 * (b % 4) + 512), k == 0, k == KD - 1)
                    if i == N_OUT - 1 and b == 3:
                        last.then_inc(out_first, 1)
                last.then_inc(tile_done, 1)

            ahead = 2
            for half in range(2):
                pe.wait_ge(zn_ready, 2 * half + 2)
                for u in range(8 + ahead):
                    m = KD * half + 2 * u
                    if u < 8:
                        if half == 0 and u < 3:
                            pe.wait_ge(z_ready, 8 + x1_bank(m) + 1)
                        elif half == 0:
                            pe.wait_ge(x1_full_act, m - 4)
                        elif u == 0:
                            pe.wait_ge(x1_full_act, KD)
                            pe.wait_ge(z_ready, 16)
                        elif u == 7:
                            pe.wait_ge(x1_full_dve, 2)
                        for kk in range(2):
                            for c in range(2):
                                last = pe.transpose(ps[:, x1_bank(m), 256 * kk + P * c:256 * kk + P * c + P],
                                                    rows[:, 2 * half + c, P * (2 * u + kk):P * (2 * u + kk) + P], ident[:, :])
                        last.then_inc(x1_turned, 1)
                    if u >= ahead:
                        for k in (2 * (u - ahead), 2 * (u - ahead) + 1):
                            if k == 0 and half == 0:
                                pe.wait_ge(tile_lo, FF0 + 1)
                            wait_x1_lo(pe, KD * half + k)
                            last = mm3(ps[:, 0, 256 * half:256 * half + 256], w_tile(FF0, P * k, P * k + P),
                                       (act_hi[:, half, k, :], act_lo[:, half, k, :]), k == 0, k == KD - 1)
            last.then_inc(tile_done, 1)

            def group(i, last_group):
                for j in range(BODY - last_group):
                    n = i * BODY + (FF0 + 1 + j)
                    if j < (7 if last_group else 8):
                        t = (j + 1) % 8
                        if not (isinstance(i, int) and i == 0 and j == 0):
                            pe.wait_ge(ff_conv, i * 8 + j)
                        by_features(n, FF0 + 1 + j, t % 2)
                        continue
                    q = j - (7 if last_group else 8)
                    pe.wait_ge(tile_lo, n + 1)
                    if q == 0:
                        pe.wait_ge(h_l, i * 4 + (3 if last_group else 4))
                    order = [(c, f) for c in range(NS) for f in range(FCH)]
                    if last_group and q == 0:
                        order = [(c, f) for c in range(NS) for f in range(FCH - 1)] + [(c, FCH - 1) for c in range(NS)]
                    for c, f in order:
                        if f == 0:
                            pe.wait_ge(down_free, i * 16 + (4 * q + c + 1))
                        if f == FCH - 1 and q == 0 and last_group:
                            pe.wait_ge(h_l, i * 4 + 4)
                        last = mm3(ps[:, B_V + c, :], (h_hi[:, f, P * c:P * c + P], h_lo[:, f, P * c:P * c + P]),
                                   w_tile(FF0 + 1 + j, 512 * f, 512 * f + 512), f == 0, f == FCH - 1)
                        if f == FCH - 1:
                            last.then_inc(down_done if c < NS - 1 else tile_done, 1)

            with pe.Fori(0, GROUPS - 1) as i:
                group(i, False)
            group(GROUPS - 1, True)


_SHAPES = [("x_t", (KD, P, SEQ)), ("x_rows", (NS, P, D)), ("w_mix", (N_MIX, P, TW)), ("w_out", (D, D)),
           ("w_up", (2 * D_FF // P, P, TW)), ("w_down", (D_FF // P, P, TW)), ("b_gates", (HEADS, 2)),
           ("conv_w", (P, 8, 3)), ("gain", (P, 8)), ("ln1_cols", (P, 2, KD)), ("ffn_conv", (P, 2 * D_FF // P * 4)),
           ("ln1_rows", (2, D)), ("ln2_rows", (2, D)), ("ident_in", (P, P)), ("head_rows_in", (HEADS, HEADS, P)),
           ("causal_in", (P, P))]


def kernel(**inputs):
    import numpy as np
    import concourse.bacc as bacc
    from concourse.bass_utils import run_bass_kernel_spmd

    a = {k: np.asarray(v) for k, v in inputs.items()}
    f32 = np.float32

    def by_feature_tile(w):
        return w.reshape(KD, P, P).transpose(1, 0, 2).reshape(P, TW)

    def by_position_tile(w):
        return w.reshape(4, P, 512).transpose(1, 0, 2).reshape(P, TW)

    w_in = a["w_in"][0]
    at = {"b": 0, "c": W_CONV, "h": 2 * W_CONV, "q": 3 * W_CONV, "k": 3 * W_CONV + W_ML,
          "v": 3 * W_CONV + 2 * W_ML, "o": 3 * W_CONV + 3 * W_ML, "g": 3 * W_CONV + 4 * W_ML}
    mix = np.zeros((N_MIX, P, TW), f32)
    for n, kind in enumerate(MIX):
        if kind[0] == "gates":
            w = np.zeros((D, P), f32)
            w[:, 0:HEADS] = w_in[:, at["g"]:at["g"] + HEADS]
            w[:, 32:32 + HEADS] = w_in[:, at["g"] + HEADS:at["g"] + 2 * HEADS]
            mix[n] = by_feature_tile(w)
        elif kind[0] in ("v", "o"):
            c = at[kind[0]] + kind[1] * 512
            mix[n] = by_position_tile(w_in[kind[2] * 512:kind[2] * 512 + 512, c:c + 512])
        else:
            c = at["qk"[kind[2] // 2]] + kind[1] * HD + kind[2] % 2 * P if kind[0] == "qk" \
                else at["chb"[kind[2]]] + kind[1] * P
            mix[n] = by_feature_tile(w_in[:, c:c + P])
    nf = D_FF // P
    w_up = a["w_up"][0].reshape(KD, P, 2, nf, P).transpose(3, 2, 1, 0, 4).reshape(2 * nf, P, TW)
    w_down = a["w_down"][0].reshape(GROUPS, FCH, P, 4, 512).transpose(0, 3, 2, 1, 4).reshape(nf, P, TW)
    pars = np.concatenate([a["w_ffn_conv"][0], a["b_ffn_conv"]], 0)
    ffn_conv = pars.reshape(4, 2, nf, P).transpose(3, 2, 1, 0).reshape(P, 2 * nf * 4)
    head_rows = np.zeros((HEADS, HEADS, P), f32)
    for h in range(HEADS):
        head_rows[h, h] = 1.0
    arrays = {
        "x_t": a["x"][0].T.reshape(KD, P, SEQ),
        "x_rows": a["x"][0].reshape(NS, P, D),
        "w_mix": mix, "w_out": a["w_out"][0], "w_up": w_up, "w_down": w_down,
        "b_gates": a["b_gates"][0].reshape(2, HEADS).T,
        "conv_w": a["w_sc_conv"][0].reshape(3, 8, P).transpose(2, 1, 0),
        "gain": a["mh_gain"][0].reshape(8, P).T,
        "ln1_cols": np.stack([a["ln1_g"][0], a["ln1_b"][0]]).reshape(2, KD, P).transpose(2, 0, 1),
        "ffn_conv": ffn_conv,
        "ln1_rows": np.stack([a["ln1_g"][0], a["ln1_b"][0]]),
        "ln2_rows": np.stack([a["ln2_g"][0], a["ln2_b"][0]]),
        "ident_in": np.eye(P, dtype=f32),
        "head_rows_in": head_rows,
        "causal_in": np.triu(np.ones((P, P), f32)),
    }
    nc = bacc.Bacc("TRN2", target_bir_lowering=False, num_devices=1)
    args, given = [], {}
    for name, shape in _SHAPES:
        given[name] = np.ascontiguousarray(arrays[name])
        assert given[name].shape == shape, name
        args.append(nc.dram_tensor(name, shape, F32, kind="ExternalInput").ap())
    out = nc.dram_tensor("out", (SEQ, D), F32, kind="ExternalOutput").ap()
    build(nc, *args, out)
    r = run_bass_kernel_spmd(nc, [given], core_ids=[0])
    return r.results[0]["out"].reshape(1, SEQ, D)
```

```python
from contextlib import ExitStack

import concourse.bass as bass
from concourse import mybir

F32 = mybir.dt.float32
F32R = mybir.dt.float32r
ALU = mybir.AluOpType
ACT = mybir.ActivationFunctionType

P = 128
SEQ, D, W_CONV, W_ML, D_FF = 512, 2048, 1024, 1024, 5632
HEADS = 4
HD = W_ML // HEADS
TW = 2048
KD = D // P
NS = SEQ // P
ALPHA = 2.0 ** 0.25
LN_EPS, HEAD_EPS = 1e-5, 1e-6
Q_SCALE = float(HD) ** -0.5
RAW, SPLIT = 3, 2
FCH = 4
GROUPS = D_FF // P // FCH
BODY = 3 * FCH
TAIL = [896, 960, 1152, 1536]
TAIL_PARTS = [(0, 0, TAIL[0]), (1, 0, TAIL[1]), (2, 0, TAIL[2]), (3, 0, 896), (3, 896, TAIL[3])]
LAST_DOWN = [(0, 2), (1, 2), (0, 3), (1, 3), (2, 2), (2, 3), (3, 2), (3, 3)]
FINISH_AT = [3, 4, 6, 7]

MIX = []
for _pair in range(HEADS // 2):
    MIX += [("v", _pair, q) for q in range(4)] + [("o", _pair, q) for q in range(4)]
    if _pair == 0:
        MIX += [("gates",)]
    MIX += [("qk", 2 * _pair + s, j) for s in range(2) for j in range(4)]
MIX += [("conv", c, j) for c in range(W_CONV // P) for j in range(3)]
N_MIX = len(MIX)
N_OUT = 2 * KD
OUT0 = N_MIX
FF0 = N_MIX + N_OUT
GR0 = FF0 + 2
CONV0 = MIX.index(("conv", 0, 0))
GATES = MIX.index(("gates",))
CONV_PEELED = 2
CONV_LOOP0 = CONV0 + 3 * CONV_PEELED
CONV_TURNS = (W_CONV // P - CONV_PEELED) // 2
assert CONV_LOOP0 % RAW == 0 and FF0 % RAW == 2 and FF0 % SPLIT == 1 and BODY % 6 == 0
LAST_QK = {MIX.index(("qk", h, 3)): h for h in range(HEADS)}


def window():
    steps, second = [], 0
    for m in range(0, 2 * KD, 2):
        half, k = m // KD, m % KD
        ahead = {0: [0, 2, 4], KD: range(KD, KD + 10, 2)}.get(m, [m + (8 if half else 4)])
        steps += [("turn", a) for a in ahead if a < KD * (half + 1)]
        if m == KD:
            steps += [(1, a) for a in range(second, KD)]
            second = KD
        steps += [(0, m), (0, m + 1)]
        for _ in range(SECOND[half][k // 2]):
            steps.append((1, second))
            second += 1
    return steps + [(1, m) for m in range(second, 2 * KD)]


SECOND = [[0, 0, 0, 2, 2, 2, 2, 2], [0, 0, 0, 0, 1, 1, 1, 1]]
WINDOW = window()
LAST_OUT = [2, 3, 0, 4, 1, 5, 6, 7]
B_O, B_S, B_V, B_GATES, B_TURN = 0, 2, 4, 7, 1
X_PARTS = [(0, 1), (1, 2), (2, 4), (4, 8), (8, 12), (12, 16)]
SC_AT = [0, 512, 896, 1152]
SC_W = [SEQ - P * j for j in range(NS)]
SC_ALL = sum(SC_W)
Y_CONV = 4096
G_X0, G_X1, G_T1, G_T2 = Y_CONV, Y_CONV + 768, Y_CONV + 1536, Y_CONV + 2048
HN_AT = Y_CONV + 1792
SC_BUF = Y_CONV + 4096 - SC_ALL


def build(nc, x_t, x_rows, w_mix, w_out, w_up, w_down, b_gates, conv_w, gain, ln1_cols, ffn_conv,
          ln1_rows, ln2_rows, ident_in, head_rows_in, causal_in, out):
    ctx = ExitStack()
    with ctx:
        def sb(name, shape, dt=F32, scope=ctx):
            return scope.enter_context(nc.sbuf_tensor(name, shape, dt))

        def sem(name):
            return ctx.enter_context(nc.semaphore(name))

        raw = sb("raw", [P, RAW, TW])
        w_hi = sb("w_hi", [P, SPLIT, TW], F32R)
        w_lo = sb("w_lo", [P, SPLIT, TW], F32R)
        act_hi = sb("act_hi", [P, 2, KD, 256], F32R)
        act_lo = sb("act_lo", [P, 2, KD, 256], F32R)
        stream = sb("stream", [P, NS * D])
        ident = sb("ident", [P, P])
        causal = sb("causal", [P, P])
        head_rows = sb("head_rows", [HEADS, HEADS, P])
        bg = sb("bg", [HEADS, 2])
        cw = sb("cw", [P, 8, 3])
        gain_c = sb("gain_c", [P, 8])
        ln1_c = sb("ln1_c", [P, 2, KD])
        fc = sb("fc", [P, 2 * D_FF // P * 4])
        gate_cols = sb("gate_cols", [P, 2, NS, HEADS])
        den = sb("den", [P, 4, NS])
        bstat = sb("bstat", [P, NS, 4, 6])
        mv = sb("mv", [P, NS, 2])
        std = sb("std", [P, NS])
        rstd = sb("rstd", [P, NS])
        nbias = sb("nbias", [P, NS])
        eps = sb("eps", [P, 2])
        uc = sb("uc", [P, 2 + SEQ])
        ut = sb("ut", [P, SEQ])
        ux = sb("ux", [P, SEQ])
        with ExitStack() as stage:
            v_hi = sb("v_hi", [P, NS, 2, HD + 2], F32R, stage)
            v_lo = sb("v_lo", [P, NS, 2, HD + 2], F32R, stage)
            qk_hi = sb("qk_hi", [P, 4, SEQ], F32R, stage)
            qk_lo = sb("qk_lo", [P, 4, SEQ], F32R, stage)
            p_hi = sb("p_hi", [P, SC_ALL], F32R, stage)
            p_lo = sb("p_lo", [P, SC_ALL], F32R, stage)
        with ExitStack() as stage:
            ym_hi = sb("ym_hi", [P, 8, SEQ], F32R, stage)
            ym_lo = sb("ym_lo", [P, 8, SEQ], F32R, stage)
        with ExitStack() as stage:
            h_hi = sb("h_hi", [P, FCH, SEQ], F32R, stage)
            h_lo = sb("h_lo", [P, FCH, SEQ], F32R, stage)
            x1_full = sb("x1_full", [P, 4, SEQ], F32, stage)
            f_val, f_gate, f_silu, f_prod = (x1_full[:, j, :] for j in range(4))
            ln_rows = sb("ln_rows", [P, 2, D], F32, stage)
        ps = ctx.enter_context(nc.psum_tensor("ps", [P, 8, 512], F32))

        g_x0, g_x1 = (stream[0:HEADS, g:g + 768] for g in (G_X0, G_X1))
        g_t1, g_t2 = (stream[0:HEADS, g:g + 512] for g in (G_T1, G_T2))
        hn = stream[:, HN_AT:HN_AT + NS * HD].rearrange("p (c e) -> p c e", c=NS)
        sc = stream[:, SC_BUF:SC_BUF + SC_ALL]
        y_ml = stream[:, 0:4096].rearrange("p (c e) -> p c e", c=NS)
        y_cv = stream[:, Y_CONV:Y_CONV + 4096].rearrange("p (k t) -> p k t", k=8)
        x_raw = stream[:, :].rearrange("p (k t) -> p k t", k=KD)
        rows = stream[:, :].rearrange("p (c n) -> p c n", c=NS)

        consts_in = sem("consts_in")
        x_in = [sem(f"x_in{i}") for i in range(len(X_PARTS))]
        first_in = [sem(f"first_in{i}") for i in range(4)]
        first_hi, first_lo = sem("first_hi"), sem("first_lo")
        raw_in = [sem(f"raw_in{i}") for i in range(RAW)]
        res_in = [sem(f"res_in{i}") for i in range(2)]
        ln1_in = sem("ln1_in")
        ln2_in = sem("ln2_in")
        x_hi, x_lo = sem("x_hi"), sem("x_lo")
        tile_hi, tile_lo, tile_done = sem("tile_hi"), sem("tile_lo"), sem("tile_done")
        pads = sem("pads")
        gate_lo, gate_dve, gate_act = sem("gate_lo"), sem("gate_dve"), sem("gate_act")
        gates_ready, gate_turned, gate_cols_ready = sem("gates_ready"), sem("gate_turned"), sem("gate_cols_ready")
        vp_hi, vp_lo, o_sig = sem("vp_hi"), sem("vp_lo"), sem("o_sig")
        qk_h, qk_l = sem("qk_h"), sem("qk_l")
        g_spread, decay_arg, decay_exp, decay_ready = sem("g_spread"), sem("decay_arg"), sem("decay_exp"), sem("decay_ready")
        scores_done, p_raw, p_h, p_l = sem("scores_done"), sem("p_raw"), sem("p_h"), sem("p_l")
        pv_done, norm_step, head_read = sem("pv_done"), sem("norm_step"), sem("head_read")
        head_var, head_std, y_ready = sem("head_var"), sem("head_std"), sem("y_ready")
        y_turned, ym_h, ym_l = sem("y_turned"), sem("ym_h"), sem("ym_l")
        conv_c, conv_u, conv_step, conv_y = sem("conv_c"), sem("conv_u"), sem("conv_step"), sem("conv_y")
        yc_h, yc_l = sem("yc_h"), sem("yc_l")
        z_ready, ln_step, ln_var, ln_std, zn_ready = sem("z_ready"), sem("ln_step"), sem("ln_var"), sem("ln_std"), sem("zn_ready")
        out_first = sem("out_first")
        x1_turned, x1_full_act, x1_full_dve = sem("x1_turned"), sem("x1_full_act"), sem("x1_full_dve")
        x1_h, x1_lo_pool, x1_lo_dve = sem("x1_h"), sem("x1_lo_pool"), sem("x1_lo_dve")
        rstd_step = sem("rstd_step")
        pool_step, res_ready = sem("pool_step"), sem("res_ready")
        ff_step, ff_conv, silu_done, prod_ready = sem("ff_step"), sem("ff_conv"), sem("silu_done"), sem("prod_ready")
        h_h, h_l, down_done, down_free = sem("h_h"), sem("h_l"), sem("down_done"), sem("down_free")
        tail_bias, tail_normed, tail_step = sem("tail_bias"), sem("tail_normed"), sem("tail_step")
        gained, out_dve, out_pool, stored = sem("gained"), sem("out_dve"), sem("out_pool"), sem("stored")

        def x1_piece(m):
            return x1_full[:, m % 8 // 2, m % 2 * 256:m % 2 * 256 + 256]

        def full_on_act(m):
            return m < KD or m // 2 % 3 == 0

        def wait_x1_full(eng, m):
            on_act = full_on_act(m)
            eng.wait_ge(x1_full_act if on_act else x1_full_dve,
                        sum(full_on_act(a) == on_act for a in range(m + 1)))

        def wait_x1_lo(eng, m):
            if m < KD or m % 2 == 0:
                eng.wait_ge(x1_lo_pool, m + 1 if m < KD else KD + (m - KD) // 2 + 1)
            else:
                eng.wait_ge(x1_lo_dve, (m - KD) // 2 + 1)

        def down_bank(c, q, last):
            return c if last and q == 3 else B_V + c

        def x1_bank(m):
            return 2 + m // 2 % 3 if m < KD else 2 + (m - KD) // 2 % 6

        block = ctx.enter_context(nc.Block())

        def conv_terms(eng, dst, src, pars, step, count):
            eng.tensor_scalar(dst[:, :], src[:, :], pars[2], pars[3], ALU.mult, ALU.add).then_inc(step, 1)
            for lag in (1, 2):
                eng.wait_ge(step, count + lag)
                last = eng.scalar_tensor_tensor(dst[:, lag:SEQ], src[:, 0:SEQ - lag], pars[2 - lag],
                                                dst[:, lag:SEQ], ALU.mult, ALU.add)
                if lag == 1:
                    last.then_inc(step, 1)
            return last

        @block.sync
        def _(sp):
            def load(src, n, s):
                if not (isinstance(n, int) and n < RAW):
                    sp.wait_ge(tile_lo, n - RAW + 1)
                sp.dma_start(raw[:, s % RAW, :], src).then_inc(raw_in[s % RAW], 16)

            def load_x(i):
                a, b = X_PARTS[i]
                sp.dma_start(x_raw[:, a:b, :], x_t[a:b].rearrange("k p t -> p k t")).then_inc(x_in[i], 16)

            def load_first(q):
                sp.dma_start(raw[:, 0, 512 * q:512 * q + 512], w_mix[0][:, 512 * q:512 * q + 512]).then_inc(first_in[q], 16)

            load_first(0)
            load_x(0)
            load_x(1)
            load_first(1)
            load_x(2)
            load_first(2)
            load_first(3)
            load_x(3)
            load(w_mix[1], 1, 1)
            load_x(4)
            load(w_mix[2], 2, 2)
            load_x(5)
            for n in range(3, CONV_LOOP0):
                load(w_mix[n], n, n)
            with sp.Fori(0, CONV_TURNS) as i:
                for j in range(6):
                    load(w_mix[bass.ds(i * 6 + (CONV_LOOP0 + j), 1)].rearrange("o p n -> (o p) n"),
                         i * 6 + (CONV_LOOP0 + j), CONV_LOOP0 + j)
            for i in range(N_OUT):
                k = i % KD
                r = W_CONV + k * P if k < 8 else (k - 8) * P
                load(w_out[r:r + P, :], OUT0 + i, OUT0 + i)
            load(w_up[0], FF0, FF0)
            load(w_up[1], FF0 + 1, FF0 + 1)

            def group(i, last):
                for j in range(6 if last else 8):
                    src = w_up[8 * i + 2 + j] if last else w_up[bass.ds(i * 8 + (2 + j), 1)].rearrange("o p n -> (o p) n")
                    load(src, i * BODY + (GR0 + j), GR0 + j)
                for j in range(4):
                    at = (6 if last else 8) + j
                    src = w_down[4 * i + j] if last else w_down[bass.ds(i * 4 + j, 1)].rearrange("o p n -> (o p) n")
                    load(src, i * BODY + (GR0 + at), GR0 + at)

            with sp.Fori(0, GROUPS - 1) as i:
                group(i, False)
            group(GROUPS - 1, True)
            sp.wait_ge(res_ready, NS)
            for r in range(2):
                sp.dma_start(ln_rows[:, r, :], ln2_rows[r].partition_broadcast(P)).then_inc(ln2_in, 16)
            for n, (c, a, b) in enumerate(TAIL_PARTS):
                if c == NS - 1 and b == TAIL[c]:
                    sp.wait_ge(out_pool, NS)
                    sp.dma_start(out[c * P:(c + 1) * P, b:D], rows[:, c, b:D]).then_inc(stored, 16)
                sp.wait_ge(out_dve, n + 1)
                sp.dma_start(out[c * P:(c + 1) * P, a:b], rows[:, c, a:b]).then_inc(stored, 16)
                if c < NS - 1:
                    sp.wait_ge(out_pool, c + 1)
                    sp.dma_start(out[c * P:(c + 1) * P, b:D], rows[:, c, b:D]).then_inc(stored, 16)
            sp.wait_ge(stored, 16 * (len(TAIL_PARTS) + NS))

        @block.gpsimd
        def _(pool):
            pool.memset(v_hi[:, :, :, HD:HD + 2].bitcast(F32), 1.0).then_inc(pads, 1)
            pool.memset(uc[:, 0:2], 0.0).then_inc(pads, 1)
            pool.memset(v_lo[:, :, :, HD:HD + 2].bitcast(F32), 0.0).then_inc(pads, 1)
            pool.memset(eps[:, 0:1], HEAD_EPS).then_inc(pads, 1)
            pool.memset(eps[:, 1:2], LN_EPS).then_inc(pads, 1)
            for dst, src in ((ident[:, :], ident_in), (causal[:, :], causal_in), (bg[:, :], b_gates),
                             (head_rows[:, :, :], head_rows_in), (cw[:, :, :], conv_w), (gain_c[:, :], gain),
                             (ln1_c[:, :, :], ln1_cols), (fc[:, :], ffn_conv)):
                pool.dma_start(dst, src).then_inc(consts_in, 16)
            pool.wait_ge(y_turned, 8)
            pool.dma_start(rows[:, 0:2, :], x_rows[0:2].rearrange("c p n -> p c n")).then_inc(res_in[0], 16)
            pool.wait_ge(yc_l, 8)
            pool.dma_start(rows[:, 2:4, :], x_rows[2:4].rearrange("c p n -> p c n")).then_inc(res_in[1], 16)
            pool.wait_ge(tile_done, FF0)
            for r in range(2):
                pool.dma_start(ln_rows[:, r, :], ln1_rows[r].partition_broadcast(P)).then_inc(ln1_in, 16)
            for m in [*range(KD), *range(KD, 2 * KD, 2)]:
                pool.wait_ge(x1_h, m + 1)
                pool.tensor_tensor(act_lo[:, m // KD, m % KD, :], x1_piece(m), act_hi[:, m // KD, m % KD, :].bitcast(F32),
                                   ALU.subtract).then_inc(x1_lo_pool, 1)
            pool.wait_ge(ln1_in, 32)
            pool.tensor_scalar(ln_rows[:, :, :], ln_rows[:, :, :], ALPHA, None, ALU.mult).then_inc(pool_step, 1)
            pool.wait_ge(x1_turned, KD)
            pool.wait_ge(pool_step, 1)
            for c in range(NS):
                pool.tensor_tensor(rows[:, c, :], rows[:, c, :], ln_rows[:, 0, :], ALU.mult).then_inc(pool_step, 1)
                pool.wait_ge(pool_step, c + 2)
                pool.tensor_tensor(rows[:, c, :], rows[:, c, :], ln_rows[:, 1, :], ALU.add).then_inc(res_ready, 1)
            pool.wait_ge(ln2_in, 32)
            for c in range(NS):
                part = rows[:, c, TAIL[c]:D]
                pool.wait_ge(tail_normed, c + 1)
                pool.tensor_tensor(part, part, ln_rows[:, 0, TAIL[c]:D], ALU.mult).then_inc(tail_step, 1)
                pool.wait_ge(tail_step, c + 1)
                pool.tensor_tensor(part, part, ln_rows[:, 1, TAIL[c]:D], ALU.add).then_inc(out_pool, 1)

        @block.scalar
        def _(act):
            def split(n, s, third):
                act.wait_ge(raw_in[s % RAW], third * 16 + (16 if s % RAW else 0))
                if not (isinstance(n, int) and n < SPLIT):
                    act.wait_ge(tile_done, n - SPLIT + 1)
                act.activation(w_hi[:, s % SPLIT, :], raw[:, s % RAW, :], ACT.Copy).then_inc(tile_hi, 1)

            def split_first(q):
                act.wait_ge(first_in[q], 16)
                act.activation(w_hi[:, 0, 512 * q:512 * q + 512], raw[:, 0, 512 * q:512 * q + 512],
                               ACT.Copy).then_inc(first_hi, 1)

            def split_x(k):
                for i, (a, b) in enumerate(X_PARTS):
                    if k == a:
                        act.wait_ge(x_in[i], 16)
                act.activation(act_hi[:, :, k, :], x_raw[:, k, :].rearrange("p (a t) -> p a t", a=2),
                               ACT.Copy).then_inc(x_hi, 1)

            def mix_work(n):
                kind = MIX[n]
                h = LAST_QK.get(n)
                if n == GATES:
                    act.wait_ge(gate_dve, 5)
                    act.activation(g_x1[:, 256:768], g_x1[:, 256:768], ACT.Exp, scale=-1.0).then_inc(gate_act, 1)
                    act.wait_ge(gate_act, 1)
                    act.activation(g_x1[:, 256:768], g_x1[:, 256:768], ACT.Ln, bias=1.0).then_inc(gate_act, 1)
                if kind[0] == "v" and kind[2] == 3:
                    act.wait_ge(tile_done, n + 1)
                    if kind[1]:
                        act.wait_ge(pv_done, 2 * NS * kind[1])
                    for c in range(NS):
                        act.activation(v_hi[:, c, :, 0:HD], ps[:, B_V + c, :].rearrange("p (h e) -> p h e", h=2),
                                       ACT.Copy).then_inc(vp_hi, 1)
                if kind[0] == "o" and kind[2] == 3:
                    act.wait_ge(tile_done, n + 1)
                    for c in range(NS):
                        act.activation(y_ml[:, c, kind[1] * 512:kind[1] * 512 + 512], ps[:, B_O + c, :],
                                       ACT.Sigmoid).then_inc(o_sig, 1)
                if kind[0] == "qk":
                    act.wait_ge(tile_done, n + 1)
                    act.wait_ge(scores_done, NS * kind[1]) if kind[1] else None
                    act.activation(qk_hi[:, kind[2], :], ps[:, B_V + kind[2], :], ACT.Copy).then_inc(qk_h, 1)
                if n == GATES + 3:
                    act.wait_ge(gate_dve, 28)
                    act.activation(g_t2, g_t2, ACT.Exp, scale=-1.0).then_inc(gate_act, 1)
                if h is not None:
                    act.wait_ge(decay_arg, h + 1)
                    act.activation(sc, sc, ACT.Exp, scale=-1.0).then_inc(decay_exp, 1)
                if n - 1 in LAST_QK:
                    h = LAST_QK[n - 1]
                    act.wait_ge(p_raw, NS * (h + 1))
                    if h:
                        act.wait_ge(pv_done, NS * h)
                    act.activation(p_hi[:, :], sc, ACT.Copy).then_inc(p_h, 1)
                if n - 2 in LAST_QK:
                    act.wait_ge(head_var, LAST_QK[n - 2] + 1)
                    act.activation(std[:, :], mv[:, :, 1], ACT.Sqrt, bias=eps[:, 0:1]).then_inc(head_std, 1)

            def conv_work(chunk, part):
                if part == 0:
                    act.wait_ge(tile_done, chunk * 3 + (CONV0 + 1))
                    if not isinstance(chunk, int) or chunk > 0:
                        act.wait_ge(conv_u, chunk)
                    act.activation(ux[:, :], ps[:, B_V, :], ACT.Copy).then_inc(conv_c, 1)

            def turn_y(m):
                act.wait_ge(y_turned, m + 1)
                act.activation(ym_hi[:, m, :], ps[:, m % 4, :], ACT.Copy, scale=gain_c[:, m:m + 1]).then_inc(ym_h, 1)

            act.wait_ge(pads, 5)
            act.activation(std[:, 0:1], eps[:, 0:1], ACT.Copy)
            split_first(0)
            split_x(0)
            split_x(1)
            split_first(1)
            split_x(2)
            split_x(3)
            split_first(2)
            split_first(3)
            act.wait_ge(first_hi, 4)
            act.sem_inc(tile_hi, 1)
            for k in range(4, 8):
                split_x(k)
            split(1, 1, 0)
            act.wait_ge(consts_in, 16 * 8)
            for n in range(CONV_LOOP0):
                if n < 2:
                    for k in range(8 + 4 * n, 12 + 4 * n):
                        split_x(k)
                split(n + 2, n + 2, (n + 2) // 3)
                if n >= CONV0:
                    if n - 1 in LAST_QK or n - 2 in LAST_QK:
                        mix_work(n)
                    conv_work(*MIX[n][1:])
                else:
                    mix_work(n)
                if n == CONV_LOOP0 - 2:
                    for m in range(4):
                        turn_y(m)
                if n == CONV_LOOP0 - 1:
                    for m in range(4, 8):
                        turn_y(m)
            with act.Fori(0, CONV_TURNS) as i:
                for j in range(6):
                    split(i * 6 + (CONV_LOOP0 + j + 2), CONV_LOOP0 + j + 2, i * 2 + (CONV_LOOP0 + j + 2) // 3)
                    conv_work(i * 2 + (CONV_PEELED + j // 3), j % 3)
            def ln_sqrt(done, first, last):
                act.wait_ge(ln_var, done)
                act.activation(std[:, first:last], mv[:, first:last, 1], ACT.Sqrt, bias=eps[:, 1:2]).then_inc(ln_std, 1)

            for i in range(N_OUT - 1):
                n = OUT0 + i + 2
                split(n, n, n // 3)
                if i == KD + 2:
                    ln_sqrt(1, 0, 2)
                if i < 8:
                    act.wait_ge(tile_done, OUT0)
                    act.wait_ge(conv_y, 8)
                    act.activation(act_hi[:, :, i, :], y_cv[:, i, :].rearrange("p (a t) -> p a t", a=2),
                                   ACT.Copy).then_inc(yc_h, 1)
            def x1_full_piece(m):
                act.wait_ge(x1_turned, m // 2 + 1)
                if m >= 8:
                    wait_x1_lo(act, m - 8)
                act.activation(x1_piece(m), ps[:, x1_bank(m), m % 2 * 256:m % 2 * 256 + 256], ACT.Identity,
                               bias=ln1_c[:, 1, m % KD:m % KD + 1], scale=ln1_c[:, 0, m % KD:m % KD + 1]).then_inc(x1_full_act, 1)

            def x1_hi_piece(m):
                wait_x1_full(act, m)
                act.activation(act_hi[:, m // KD, m % KD, :], x1_piece(m), ACT.Copy).then_inc(x1_h, 1)

            for m in range(KD + 1):
                if m == 4:
                    split(FF0 + 1, FF0 + 1, (FF0 + 1) // 3)
                if m < KD:
                    x1_full_piece(m)
                if m:
                    x1_hi_piece(m - 1)
                if m == 11:
                    ln_sqrt(2, 2, 4)
            for m in range(KD, 2 * KD):
                if m % 2 == 0 and m + 2 < 2 * KD and full_on_act(m + 2):
                    x1_full_piece(m + 2)
                    x1_full_piece(m + 3)
                x1_hi_piece(m)

            def hidden(i, pair):
                act.wait_ge(ff_conv, i * 8 + (2 * pair + 2))
                act.activation(f_silu[:, :], f_gate[:, :], ACT.Silu).then_inc(silu_done, 1)
                act.wait_ge(prod_ready, i * 4 + (pair + 1))
                if pair == 0:
                    act.wait_ge(tile_done, i * BODY + GR0)
                act.activation(h_hi[:, pair, :], f_prod[:, :], ACT.Copy).then_inc(h_h, 1)

            def group(i, last):
                hidden(i, 0)
                for j in range(BODY - 2 * last):
                    if not (last and j >= BODY - 4):
                        s = GR0 + j + 2
                        split(i * BODY + s, s, i * 4 + s // 3)
                    if j < 6 and j % 2:
                        hidden(i, j // 2 + 1)
            split(GR0, GR0, GR0 // 3)
            split(GR0 + 1, GR0 + 1, (GR0 + 1) // 3)
            with act.Fori(0, GROUPS - 1) as i:
                group(i, False)
            group(GROUPS - 1, True)
            for c in range(NS):
                ln_sqrt(3 + c, c, c + 1)
                act.wait_ge(tail_bias, c + 1)
                part = rows[:, c, TAIL[c]:D]
                act.activation(part, part, ACT.Identity, bias=nbias[:, c:c + 1],
                               scale=rstd[:, c:c + 1]).then_inc(tail_normed, 1)

        @block.vector
        def _(dve):
            def split(n, s):
                dve.wait_ge(tile_hi, n + 1)
                if isinstance(n, int) and n == GATES:
                    both, src = (w[:, slot, :].rearrange("p (k n) -> p k n", k=KD)[:, :, P // 2:P]
                                 for w, slot in ((w_hi, s % SPLIT), (raw, s % RAW)))
                    dve.tensor_tensor(both, src, both.bitcast(F32), ALU.subtract).then_inc(tile_lo, 1)
                    return
                dve.tensor_tensor(w_lo[:, s % SPLIT, :], raw[:, s % RAW, :], w_hi[:, s % SPLIT, :].bitcast(F32),
                                  ALU.subtract).then_inc(tile_lo, 1)

            def split_first(q):
                dve.wait_ge(first_hi, q + 1)
                at = slice(512 * q, 512 * q + 512)
                dve.tensor_tensor(w_lo[:, 0, at], raw[:, 0, at], w_hi[:, 0, at].bitcast(F32), ALU.subtract).then_inc(first_lo, 1)

            def split_x(k):
                dve.wait_ge(x_hi, k + 1)
                dve.tensor_tensor(act_lo[:, :, k, :], x_raw[:, k, :].rearrange("p (a t) -> p a t", a=2),
                                  act_hi[:, :, k, :].bitcast(F32), ALU.subtract).then_inc(x_lo, 1)

            def doubling(first, last, op, count):
                for s in range(first, last):
                    src, dst = (g_x0, g_x1) if s % 2 == 0 else (g_x1, g_x0)
                    dve.wait_ge(gate_dve, count + s - first)
                    dve.tensor_tensor(dst[:, 256:768], src[:, 256:768], src[:, 256 - 2 ** s:768 - 2 ** s],
                                      op).then_inc(gate_dve, 1)

            def gates_a():
                dve.wait_ge(consts_in, 16 * 8)
                dve.wait_ge(tile_done, GATES + 1)
                dve.tensor_copy(g_x0[:, 256:768], ps[64:64 + HEADS, B_GATES, :]).then_inc(gate_lo, 1)
                dve.tensor_copy(g_x1[:, 256:768], ps[96:96 + HEADS, B_GATES, :]).then_inc(gate_lo, 1)
                dve.wait_ge(gate_lo, 2)
                dve.scalar_tensor_tensor(g_t1, ps[0:HEADS, B_GATES, :], bg[:, 0:1], g_x0[:, 256:768], ALU.add,
                                         ALU.add).then_inc(gate_dve, 1)
                dve.tensor_copy(g_t2, ps[32:32 + HEADS, B_GATES, :]).then_inc(gate_dve, 1)
                dve.memset(g_x0[:, 0:256], 0.0)
                dve.memset(g_x1[:, 0:256], 0.0).then_inc(gate_dve, 1)
                dve.wait_ge(gate_dve, 2)
                dve.scalar_tensor_tensor(g_t2, g_t2, bg[:, 1:2], g_x1[:, 256:768], ALU.add, ALU.add).then_inc(gate_dve, 1)
                dve.wait_ge(gate_dve, 4)
                dve.scalar_tensor_tensor(g_x1[:, 256:768], g_t2, -1.0, g_t2, ALU.mult, ALU.max).then_inc(gate_dve, 1)

            def gates_b():
                dve.wait_ge(gate_act, 2)
                dve.scalar_tensor_tensor(g_x0[:, 256:768], g_t2, 0.0, g_x1[:, 256:768], ALU.min,
                                         ALU.subtract).then_inc(gate_dve, 1)

            def gates_mid():
                dve.wait_ge(gate_dve, 15)
                dve.tensor_tensor(g_t1, g_t1, g_x1[:, 256:768], ALU.subtract).then_inc(gate_dve, 1)
                dve.tensor_copy(g_t2, g_x1[:, 256:768]).then_inc(gate_dve, 1)
                dve.wait_ge(gate_dve, 16)
                dve.tensor_copy(g_x0[:, 256:768], g_t1).then_inc(gate_dve, 1)

            def norm_heads(h):
                t = h * 13
                dve.wait_ge(pv_done, NS * (h + 1))
                dve.tensor_copy(den[:, 0, :], ps[:, 0:NS, HD]).then_inc(norm_step, 1)
                dve.wait_ge(norm_step, t + 1)
                dve.scalar_tensor_tensor(den[:, 1, :], den[:, 0, :], -1.0, den[:, 0, :], ALU.mult,
                                         ALU.max).then_inc(norm_step, 1)
                dve.wait_ge(norm_step, t + 2)
                dve.tensor_tensor(den[:, 2, :], den[:, 1, :], gate_cols[:, 1, :, h], ALU.max).then_inc(norm_step, 1)
                dve.wait_ge(norm_step, t + 3)
                dve.reciprocal(den[:, 3, :], den[:, 2, :]).then_inc(norm_step, 1)
                dve.wait_ge(norm_step, t + 4)
                for c in range(NS):
                    dve.tensor_scalar(hn[:, c, :], ps[:, c, 0:HD], den[:, 3, c:c + 1], None,
                                      ALU.mult).then_inc(head_read, 1)
                for c in range(NS):
                    dve.wait_ge(head_read, NS * h + c + 1)
                    dve.bn_stats(bstat[:, c, 0, :], hn[:, c, :]).then_inc(norm_step, 1)
                for c in range(NS):
                    dve.wait_ge(norm_step, t + 5 + c)
                    last = dve.bn_aggr(mv[:, c, :], bstat[:, c, 0, :])
                last.then_inc(head_var, 1)
                dve.wait_ge(head_std, h + 1)
                dve.reciprocal(rstd[:, :], std[:, :]).then_inc(norm_step, 1)
                dve.wait_ge(norm_step, t + 9)
                for c in range(NS):
                    dve.tensor_scalar(hn[:, c, :], hn[:, c, :], mv[:, c, 0:1], rstd[:, c:c + 1], ALU.subtract,
                                      ALU.mult).then_inc(norm_step, 1)
                for c in range(NS):
                    dve.wait_ge(norm_step, t + 10 + c)
                    dve.wait_ge(o_sig, NS * (h // 2 + 1))
                    y = y_ml[:, c, h * HD:(h + 1) * HD]
                    dve.tensor_tensor(y, y, hn[:, c, :], ALU.mult).then_inc(y_ready, 1)

            def mix_work(n):
                kind = MIX[n]
                if n - 1 in LAST_QK:
                    h = LAST_QK[n - 1]
                    dve.wait_ge(decay_ready, h + 1)
                    for j in range(NS):
                        dve.wait_ge(scores_done, NS * h + j + 1)
                        s = sc[:, SC_AT[j]:SC_AT[j] + SC_W[j]]
                        dve.scalar_tensor_tensor(s, ps[:, B_S + j % 2, 0:SC_W[j]], Q_SCALE, s, ALU.mult,
                                                 ALU.mult).then_inc(p_raw, 1)
                if n == GATES:
                    gates_a()
                if kind[0] == "v" and kind[2] == 3:
                    for c in range(NS):
                        dve.wait_ge(vp_hi, NS * kind[1] + c + 1)
                        dve.tensor_tensor(v_lo[:, c, :, 0:HD], ps[:, B_V + c, :].rearrange("p (h e) -> p h e", h=2),
                                          v_hi[:, c, :, 0:HD].bitcast(F32), ALU.subtract).then_inc(vp_lo, 1)
                if n == GATES + 4:
                    dve.wait_ge(gate_turned, 1)
                    dve.tensor_copy(gate_cols[:, :, :, :], ps[:, B_TURN, 0:32].rearrange("p (a c h) -> p a c h", a=2, c=NS)
                                    ).then_inc(gate_cols_ready, 1)
                    dve.wait_ge(gate_cols_ready, 1)
                if kind[0] == "qk":
                    dve.wait_ge(qk_h, 4 * kind[1] + kind[2] + 1)
                    dve.tensor_tensor(qk_lo[:, kind[2], :], ps[:, B_V + kind[2], :],
                                      qk_hi[:, kind[2], :].bitcast(F32), ALU.subtract).then_inc(qk_l, 1)
                h = LAST_QK.get(n)
                if h is not None:
                    dve.wait_ge(g_spread, h + 1)
                    if h:
                        dve.wait_ge(p_h, h)
                    for j in range(NS):
                        last = dve.tensor_scalar(sc[:, SC_AT[j]:SC_AT[j] + SC_W[j]], ps[:, B_S, P * j:SEQ],
                                                 gate_cols[:, 0, j, h:h + 1], 0.0, ALU.subtract, ALU.max)
                    last.then_inc(decay_arg, 1)

            def mix_work_b(n):
                h = LAST_QK.get(n)
                if n == GATES:
                    gates_b()
                if n == GATES + 1:
                    doubling(0, 9, ALU.add, 6)
                    gates_mid()
                if n == GATES + 2:
                    doubling(0, 9, ALU.max, 18)
                if n == GATES + 3:
                    dve.wait_ge(gate_dve, 27)
                    dve.tensor_tensor(g_t2, g_t2, g_x1[:, 256:768], ALU.add).then_inc(gate_dve, 1)
                    dve.wait_ge(gate_act, 3)
                    dve.sem_inc(gates_ready, 1)
                if h is not None:
                    dve.wait_ge(decay_exp, h + 1)
                    for j in range(NS):
                        d = sc[:, SC_AT[j]:SC_AT[j] + P]
                        last = dve.tensor_tensor(d, d, causal[:, :], ALU.mult)
                    last.then_inc(decay_ready, 1)
                if n - 1 in LAST_QK:
                    h = LAST_QK[n - 1]
                    dve.wait_ge(p_h, h + 1)
                    dve.tensor_tensor(p_lo[:, :], sc, p_hi[:, :].bitcast(F32), ALU.subtract).then_inc(p_l, 1)
                if n - 2 in LAST_QK:
                    norm_heads(LAST_QK[n - 2])

            def conv_work(chunk, part):
                if part == 1:
                    dve.wait_ge(tile_done, chunk * 3 + (CONV0 + 2))
                    dve.wait_ge(conv_c, chunk + 1)
                    dve.tensor_tensor(uc[:, 2:2 + SEQ], ps[:, B_V + 1, :], ux[:, :], ALU.mult).then_inc(conv_u, 1)
                    dve.wait_ge(conv_u, chunk + 1)
                    w = cw[:, chunk, :] if isinstance(chunk, int) else cw[:, bass.ds(chunk, 1), :].rearrange("p o w -> p (o w)")
                    dve.tensor_scalar(ut[:, :], uc[:, 2:2 + SEQ], w[:, 2:3], None, ALU.mult).then_inc(conv_step, 1)
                    for lag in (1, 2):
                        dve.wait_ge(conv_step, chunk * 3 + lag)
                        dve.scalar_tensor_tensor(ut[:, :], uc[:, 2 - lag:2 - lag + SEQ], w[:, 2 - lag:3 - lag], ut[:, :],
                                                 ALU.mult, ALU.add).then_inc(conv_step, 1)
                if part == 2:
                    dve.wait_ge(tile_done, chunk * 3 + (CONV0 + 3))
                    dve.wait_ge(conv_step, chunk * 3 + 3)
                    y = y_cv[:, chunk, :] if isinstance(chunk, int) else \
                        y_cv[:, bass.ds(chunk, 1), :].rearrange("p o t -> p (o t)")
                    dve.tensor_tensor(y, ps[:, B_V + 2, :], ut[:, :], ALU.mult).then_inc(conv_y, 1)

            def turn_y(m):
                dve.wait_ge(ym_h, m + 1)
                dve.scalar_tensor_tensor(ym_lo[:, m, :], ps[:, m % 4, :], gain_c[:, m:m + 1],
                                         ym_hi[:, m, :].bitcast(F32), ALU.mult, ALU.subtract).then_inc(ym_l, 1)

            split_first(0)
            split_x(0)
            split_x(1)
            split_first(1)
            split_x(2)
            split_x(3)
            split_first(2)
            split_first(3)
            dve.wait_ge(first_lo, 4)
            dve.sem_inc(tile_lo, 1)
            for k in range(4, 8):
                split_x(k)
            split(1, 1)
            for n in range(CONV_LOOP0):
                if n < 2:
                    for k in range(8 + 4 * n, 12 + 4 * n):
                        split_x(k)
                if n < CONV0 or n - 1 in LAST_QK:
                    mix_work(n)
                split(n + 2, n + 2)
                mix_work_b(n)
                if n >= CONV0:
                    if n == CONV0:
                        dve.wait_ge(pads, 3)
                    conv_work(*MIX[n][1:])
                if n == CONV_LOOP0 - 2:
                    for m in range(4):
                        turn_y(m)
                if n == CONV_LOOP0 - 1:
                    for m in range(4, 8):
                        turn_y(m)
            with dve.Fori(0, CONV_TURNS) as i:
                for j in range(6):
                    if j % 3 == 1:
                        split(i * 6 + (CONV_LOOP0 + j + 2), CONV_LOOP0 + j + 2)
                    conv_work(i * 2 + (CONV_PEELED + j // 3), j % 3)
                    if j % 3 != 1:
                        split(i * 6 + (CONV_LOOP0 + j + 2), CONV_LOOP0 + j + 2)

            def ln_stats(c):
                for q in range(4):
                    dve.bn_stats(bstat[:, c, q, :], rows[:, c, 512 * q:512 * q + 512]).then_inc(ln_step, 1)
                dve.wait_ge(ln_step, 4 * (c + 1))
                last = dve.bn_aggr(mv[:, c, :], bstat[:, c, :, :].rearrange("p a b -> p (a b)"))
                if c % 2:
                    last.then_inc(ln_var, 1)

            def ln_norm(c):
                if c % 2 == 0:
                    dve.wait_ge(ln_std, c // 2 + 1)
                    dve.reciprocal(rstd[:, c:c + 2], std[:, c:c + 2]).then_inc(rstd_step, 1)
                    dve.wait_ge(rstd_step, c // 2 + 1)
                dve.tensor_scalar(rows[:, c, :], rows[:, c, :], mv[:, c, 0:1], rstd[:, c:c + 1], ALU.subtract,
                                  ALU.mult).then_inc(zn_ready, 1)

            for i in range(N_OUT):
                n = OUT0 + i + 2
                if i < N_OUT - 2 and i != KD - 1:
                    split(n, n)
                if i < 8:
                    dve.wait_ge(yc_h, i + 1)
                    dve.tensor_tensor(act_lo[:, :, i, :], y_cv[:, i, :].rearrange("p (a t) -> p a t", a=2),
                                      act_hi[:, :, i, :].bitcast(F32), ALU.subtract).then_inc(yc_l, 1)
                if i % KD == KD - 1:
                    half = i // KD
                    dve.wait_ge(res_in[half], 16)
                    for j, b in enumerate(LAST_OUT if half else range(8)):
                        if j == 0:
                            dve.wait_ge(out_first, half + 1)
                        if j == (3 if half else 4):
                            dve.wait_ge(tile_done, OUT0 + i + 1)
                        x = rows[:, 2 * half + b // 4, 512 * (b % 4):512 * (b % 4) + 512]
                        dve.scalar_tensor_tensor(x, x, ALPHA, ps[:, b, :], ALU.mult, ALU.add).then_inc(z_ready, 1)
                        if half == 0 and j == 7:
                            split(OUT0 + KD + 1, OUT0 + KD + 1)
                        if half and j == 1:
                            split(FF0, FF0)
                if i in (KD, KD + 1):
                    dve.wait_ge(z_ready, 8)
                    ln_stats(i - KD)
                if i in (KD + 3, KD + 4):
                    ln_norm(i - KD - 3)
            split(FF0 + 1, FF0 + 1)
            dve.wait_ge(z_ready, 16)
            ln_stats(2)
            ln_stats(3)
            ln_norm(2)
            ln_norm(3)
            for k in range(KD + 2):
                m = KD + k
                if k < KD and not full_on_act(m):
                    dve.wait_ge(x1_turned, m // 2 + 1)
                    wait_x1_lo(dve, m - 8)
                    dve.tensor_scalar(x1_piece(m), ps[:, x1_bank(m), m % 2 * 256:m % 2 * 256 + 256], ln1_c[:, 0, k:k + 1],
                                      ln1_c[:, 1, k:k + 1], ALU.mult, ALU.add).then_inc(x1_full_dve, 1)
                if k >= 2 and k % 2:
                    dve.wait_ge(x1_h, m - 1)
                    dve.tensor_tensor(act_lo[:, 1, k - 2, :], x1_piece(m - 2), act_hi[:, 1, k - 2, :].bitcast(F32),
                                      ALU.subtract).then_inc(x1_lo_dve, 1)

            def up_work(i, t, static):
                dst = f_gate if t % 2 else f_val
                if static:
                    c = (8 * i + t) * 4
                    pars = [fc[:, c + r:c + r + 1] for r in range(4)]
                else:
                    pars = [fc[:, bass.ds(i * 32 + (4 * t + r), 1)] for r in range(4)]
                up = i * 8 + t
                if t % 2:
                    if not static or i or t > 1:
                        dve.wait_ge(silu_done, i * 4 + t // 2)
                elif not static or i or t:
                    dve.wait_ge(prod_ready, i * 4 + t // 2)
                last = conv_terms(dve, dst, ps[:, t % 2, :], pars, ff_step, up * 2)
                last.then_inc(ff_conv, 1)

            def hidden(i, pair):
                dve.wait_ge(silu_done, i * 4 + (pair + 1))
                dve.wait_ge(ff_conv, i * 8 + (2 * pair + 1))
                if not (isinstance(i, int) and i == 0 and pair == 0):
                    dve.wait_ge(h_h, i * 4 + pair)
                dve.tensor_tensor(f_prod[:, :], f_silu[:, :], f_val[:, :], ALU.mult).then_inc(prod_ready, 1)
                dve.wait_ge(prod_ready, i * 4 + (pair + 1))
                dve.wait_ge(h_h, i * 4 + (pair + 1))
                dve.tensor_tensor(h_lo[:, pair, :], f_prod[:, :], h_hi[:, pair, :].bitcast(F32),
                                  ALU.subtract).then_inc(h_l, 1)

            def finish(c):
                dve.wait_ge(ln_std, 3 + c)
                dve.reciprocal(rstd[:, c:c + 1], std[:, c:c + 1]).then_inc(rstd_step, 1)
                dve.wait_ge(rstd_step, 3 + c)
                dve.scalar_tensor_tensor(nbias[:, c:c + 1], mv[:, c, 0:1], -1.0, rstd[:, c:c + 1], ALU.mult,
                                         ALU.mult).then_inc(tail_bias, 1)
                dve.wait_ge(ln2_in, 32)
                for n in [n for n, part in enumerate(TAIL_PARTS) if part[0] == c]:
                    _, a, b = TAIL_PARTS[n]
                    part = rows[:, c, a:b]
                    dve.scalar_tensor_tensor(part, part, mv[:, c, 0:1], ln_rows[:, 0, a:b], ALU.subtract,
                                             ALU.mult).then_inc(gained, 1)
                    dve.wait_ge(gained, n + 1)
                    dve.scalar_tensor_tensor(part, part, rstd[:, c:c + 1], ln_rows[:, 1, a:b], ALU.mult,
                                             ALU.add).then_inc(out_dve, 1)

            def down_add(c, q, added, last):
                x = rows[:, c, 512 * q:512 * q + 512]
                dve.tensor_tensor(x, x, ps[:, down_bank(c, q, last), :], ALU.add).then_inc(down_free, 1)
                if last:
                    dve.wait_ge(down_free, added)
                    dve.bn_stats(bstat[:, c, q, :], x).then_inc(ln_step, 1)

            def group(i, last):
                hidden(i, 0)
                for j in range((BODY - 4) if last else BODY):
                    up = (j + 2) % 8
                    is_up = j < (6 if last else 8)
                    if is_up:
                        dve.wait_ge(tile_done, i * BODY + (GR0 + 1 + j))
                        up_work(i if j < 6 else i + 1, up, last)
                        if not (last and j == 5):
                            split(i * BODY + (GR0 + 2 + j), GR0 + j + 2)
                    if j < 6 and j % 2:
                        hidden(i, j // 2 + 1)
                    if last and j == 5:
                        split(i * BODY + (GR0 + 2 + j), GR0 + j + 2)
                    if not is_up:
                        q = j - (6 if last else 8)
                        if q == 0:
                            dve.wait_ge(res_ready, NS)
                        for c in range(NS):
                            if c < NS - 1:
                                dve.wait_ge(down_done, i * 12 + (3 * q + c + 1))
                            else:
                                dve.wait_ge(tile_done, i * BODY + (GR0 + 1 + j))
                            down_add(c, q, i * 16 + NS + 4 * q + c + 1, last)
                        split(i * BODY + (GR0 + 2 + j), GR0 + j + 2)
                if last:
                    for n, (c, q) in enumerate(LAST_DOWN):
                        dve.wait_ge(down_done, i * 12 + 6 + n + 1)
                        down_add(c, q, i * 16 + NS + 8 + n + 1, last)
                        if q == 3:
                            dve.wait_ge(ln_step, 16 + 8 + n + 1)
                            dve.bn_aggr(mv[:, c, :], bstat[:, c, :, :].rearrange("p a b -> p (a b)")).then_inc(ln_var, 1)
                        if n in FINISH_AT:
                            finish(FINISH_AT.index(n))

            dve.sem_inc(down_free, NS)
            dve.wait_ge(tile_done, FF0 + 1)
            up_work(0, 0, True)
            split(GR0, GR0)
            dve.wait_ge(tile_done, FF0 + 2)
            up_work(0, 1, True)
            split(GR0 + 1, GR0 + 1)
            with dve.Fori(0, GROUPS - 1) as i:
                group(i, False)
            group(GROUPS - 1, True)

        @block.tensor
        def _(pe):
            def mm3(dst, a, b, first, last):
                pe.matmul(dst, a[0], b[0], start=first, stop=False)
                pe.matmul(dst, a[0], b[1], start=False, stop=False)
                return pe.matmul(dst, a[1], b[0], start=False, stop=last)

            def w_tile(s, lo, hi):
                return w_hi[:, s % SPLIT, lo:hi], w_lo[:, s % SPLIT, lo:hi]

            def acts(k):
                return act_hi[:, :, k, :], act_lo[:, :, k, :]

            def acts_block(k, c):
                at = P * (c % 2)
                return act_hi[:, c // 2, k, at:at + P], act_lo[:, c // 2, k, at:at + P]

            def bank(b):
                return ps[:, b, :].rearrange("p (a t) -> p a t", a=2)

            def by_features(n, s, b):
                pe.wait_ge(tile_lo, n + 1)
                for k in range(KD):
                    last = mm3(bank(b), w_tile(s, P * k, P * k + P), acts(k), k == 0, k == KD - 1)
                last.then_inc(tile_done, 1)

            def gates(n):
                pe.wait_ge(tile_lo, n + 1)
                for k in range(KD):
                    w = w_hi[:, n % SPLIT, P * k:P * k + P]
                    pe.matmul(bank(B_GATES), w, act_hi[:, :, k, :], start=k == 0, stop=False)
                    last = pe.matmul(bank(B_GATES), w, act_lo[:, :, k, :], start=False, stop=k == KD - 1)
                last.then_inc(tile_done, 1)

            def by_positions(n, b, q, left=None):
                if n:
                    pe.wait_ge(tile_lo, n + 1)
                for kk in range(4):
                    k = 4 * q + kk
                    if n == 0:
                        pe.wait_ge(first_lo, kk + 1)
                    if n < 4:
                        pe.wait_ge(x_lo, k + 1)
                    for c in range(NS):
                        if left and k == 0:
                            pe.wait_ge(left[0], left[1] + c)
                        last = mm3(ps[:, b + c, :], acts_block(k, c), w_tile(n, 512 * kk, 512 * kk + 512),
                                   k == 0, k == KD - 1)
                last.then_inc(tile_done, 1)

            def spread_g(h):
                if h == 0:
                    pe.wait_ge(o_sig, NS)
                else:
                    pe.wait_ge(head_read, NS * h)
                    pe.wait_ge(o_sig, NS * (h // 2 + 1))
                pe.matmul(ps[:, B_S, :], head_rows[:, h, :], g_x1[:, 256:768], start=True, stop=True).then_inc(g_spread, 1)

            def scores(h):
                pe.wait_ge(qk_l, 4 * (h + 1))
                pe.wait_ge(decay_arg, h + 1)
                for j in range(NS):
                    if j >= 2:
                        pe.wait_ge(p_raw, NS * h + j - 1)
                    for d in range(2):
                        at = P * j
                        last = mm3(ps[:, B_S + j % 2, 0:SC_W[j]],
                                   (qk_hi[:, 2 + d, at:at + P], qk_lo[:, 2 + d, at:at + P]),
                                   (qk_hi[:, d, at:SEQ], qk_lo[:, d, at:SEQ]), d == 0, d == 1)
                    last.then_inc(scores_done, 1)

            def values(h):
                pe.wait_ge(p_l, h + 1)
                pe.wait_ge(vp_lo, NS * (h // 2 + 1))
                if h == 0:
                    pe.wait_ge(pads, 3)
                else:
                    pe.wait_ge(head_read, NS * h)
                for c in range(NS):
                    for j in range(c + 1):
                        at = SC_AT[j] + P * (c - j)
                        last = mm3(ps[:, c, 0:HD + 2], (p_hi[:, at:at + P], p_lo[:, at:at + P]),
                                   (v_hi[:, j, h % 2, :], v_lo[:, j, h % 2, :]), j == 0, j == c)
                    last.then_inc(pv_done, 1)

            def turn_gates():
                pe.wait_ge(consts_in, 16 * 8)
                pe.wait_ge(gates_ready, 1)
                pe.wait_ge(o_sig, NS)
                for a, src in enumerate((g_t1, g_t2)):
                    for c in range(NS):
                        at = (a * NS + c) * HEADS
                        last = pe.transpose(ps[:, B_TURN, at:at + HEADS], src[:, P * c:P * c + P], ident[0:HEADS, 0:HEADS])
                last.then_inc(gate_turned, 1)

            def turn_y(m):
                pe.wait_ge(y_ready, 4 * (m // 2 + 1))
                if m < 4:
                    pe.wait_ge(head_read, NS * HEADS)
                    pe.wait_ge(p_l, HEADS)
                else:
                    pe.wait_ge(ym_l, m - 3)
                for c in range(NS):
                    last = pe.transpose(ps[:, m % 4, P * c:P * c + P], y_ml[:, c, P * m:P * m + P], ident[:, :])
                last.then_inc(y_turned, 1)

            def conv_tile(n, s, chunk, part):
                if isinstance(chunk, int) and chunk == 0:
                    pe.wait_ge(qk_l, 13 + part)
                else:
                    pe.wait_ge((conv_c, conv_u, conv_y)[part], chunk)
                by_features(n, s, B_V + part)

            for n in range(CONV_LOOP0):
                kind = MIX[n]
                if kind[0] == "gates":
                    pe.wait_ge(vp_lo, NS)
                    gates(n)
                elif kind[0] == "v":
                    by_positions(n, B_V, kind[2], (qk_l, 8 * kind[1] - 3) if kind[1] else None)
                elif kind[0] == "o":
                    if kind[2] == 0 and kind[1]:
                        pe.wait_ge(head_read, 2 * NS * kind[1])
                    by_positions(n, B_O, kind[2])
                elif kind[0] == "qk":
                    _, h, j = kind
                    if h % 2 == 0:
                        pe.wait_ge(vp_lo, NS * (h // 2 + 1))
                        if B_V + j == B_GATES:
                            pe.wait_ge(gate_dve, 2)
                    else:
                        pe.wait_ge(qk_l, 4 * (h - 1) + j + 1)
                    by_features(n, n, B_V + j)
                else:
                    conv_tile(n, n, kind[1], kind[2])
                if n == GATES + 4:
                    turn_gates()
                if n in LAST_QK:
                    spread_g(LAST_QK[n])
                if n - 1 in LAST_QK:
                    scores(LAST_QK[n - 1])
                if n - 2 in LAST_QK:
                    values(LAST_QK[n - 2])
                if n == CONV_LOOP0 - 2:
                    for m in range(4):
                        turn_y(m)
                if n == CONV_LOOP0 - 1:
                    for m in range(4, 8):
                        turn_y(m)
            with pe.Fori(0, CONV_TURNS) as i:
                for j in range(6):
                    conv_tile(i * 6 + (CONV_LOOP0 + j), CONV_LOOP0 + j, i * 2 + (CONV_PEELED + j // 3), j % 3)

            for i in range(N_OUT):
                n, half, k = OUT0 + i, i // KD, i % KD
                pe.wait_ge(tile_lo, n + 1)
                if i == 0:
                    pe.wait_ge(ym_l, 8)
                if 8 <= i < KD:
                    pe.wait_ge(yc_l, k - 7)
                for b in range(8):
                    if i == KD:
                        pe.wait_ge(z_ready, b + 1)
                    if i == 0 and 0 <= b - B_V < 3:
                        pe.wait_ge((conv_c, conv_u, conv_y)[b - B_V], 8)
                    c = 2 * half + b // 4
                    y = (ym_hi[:, k, P * c:P * c + P], ym_lo[:, k, P * c:P * c + P]) if k < 8 else acts_block(k - 8, c)
                    last = mm3(ps[:, b, :], y, w_tile(n, 512 * (b % 4), 512 * (b % 4) + 512), k == 0, k == KD - 1)
                    if i % KD == KD - 1 and b == 3:
                        last.then_inc(out_first, 1)
                last.then_inc(tile_done, 1)

            for what, m in WINDOW:
                half, k = m // KD, m % KD
                if what == "turn":
                    if m == 0:
                        pe.wait_ge(zn_ready, 2)
                    if m == KD:
                        pe.wait_ge(zn_ready, 4)
                        pe.wait_ge(x1_full_act, KD)
                        pe.wait_ge(z_ready, 16)
                    if m < 6:
                        pe.wait_ge(z_ready, 8 + LAST_OUT.index(x1_bank(m)) + 1)
                    elif half == 0:
                        pe.wait_ge(x1_full_act, m - 4)
                    elif k >= 12:
                        wait_x1_full(pe, m - 12)
                        wait_x1_full(pe, m - 11)
                    for kk in range(2):
                        for c in range(2):
                            last = pe.transpose(ps[:, x1_bank(m), 256 * kk + P * c:256 * kk + P * c + P],
                                                rows[:, 2 * half + c, P * (k + kk):P * (k + kk) + P], ident[:, :])
                    last.then_inc(x1_turned, 1)
                else:
                    if m == 0:
                        pe.wait_ge(tile_lo, FF0 + what + 1)
                        pe.wait_ge(z_ready, 8 + LAST_OUT.index(what) + 1)
                    wait_x1_lo(pe, m)
                    last = mm3(ps[:, what, 256 * half:256 * half + 256], w_tile(FF0 + what, P * k, P * k + P),
                               (act_hi[:, half, k, :], act_lo[:, half, k, :]), k == 0, k == KD - 1)
                    if m == 2 * KD - 1:
                        last.then_inc(tile_done, 1)

            def down_product(s, c, f, b):
                return mm3(ps[:, b, :], (h_hi[:, f, P * c:P * c + P], h_lo[:, f, P * c:P * c + P]),
                           w_tile(s, 512 * f, 512 * f + 512), f == 0, f == FCH - 1)

            def group(i, last_group):
                ups = 6 if last_group else 8
                for j in range(ups):
                    n = i * BODY + (GR0 + j)
                    pe.wait_ge(ff_conv, i * 8 + (j + 1))
                    by_features(n, GR0 + j, j % 2)
                for q in range(2 if last_group else 4):
                    j = ups + q
                    pe.wait_ge(tile_lo, i * BODY + (GR0 + j + 1))
                    if q == 0:
                        pe.wait_ge(h_l, i * 4 + (3 if last_group else 4))
                    order = [(c, f) for c in range(NS) for f in range(FCH)]
                    if last_group and q == 0:
                        order = [(c, f) for c in range(NS) for f in range(FCH - 1)] + [(c, FCH - 1) for c in range(NS)]
                    for c, f in order:
                        if f == 0:
                            pe.wait_ge(down_free, i * 16 + (4 * q + c + 1))
                        if f == FCH - 1 and q == 0 and last_group:
                            pe.wait_ge(h_l, i * 4 + 4)
                        last = down_product(GR0 + j, c, f, B_V + c)
                        if f == FCH - 1:
                            last.then_inc(down_done if c < NS - 1 else tile_done, 1)
                if last_group:
                    for c, q in LAST_DOWN:
                        pe.wait_ge(tile_lo, i * BODY + (GR0 + ups + q + 1))
                        if q == 2:
                            pe.wait_ge(down_free, i * 16 + (4 * q + c + 1))
                        else:
                            pe.wait_ge(ff_conv, 8 * GROUPS)
                        for f in range(FCH):
                            last = down_product(GR0 + ups + q, c, f, down_bank(c, q, True))
                        last.then_inc(down_done, 1)

            with pe.Fori(0, GROUPS - 1) as i:
                group(i, False)
            group(GROUPS - 1, True)


_SHAPES = [("x_t", (KD, P, SEQ)), ("x_rows", (NS, P, D)), ("w_mix", (N_MIX, P, TW)), ("w_out", (D, D)),
           ("w_up", (2 * D_FF // P, P, TW)), ("w_down", (D_FF // P, P, TW)), ("b_gates", (HEADS, 2)),
           ("conv_w", (P, 8, 3)), ("gain", (P, 8)), ("ln1_cols", (P, 2, KD)), ("ffn_conv", (P, 2 * D_FF // P * 4)),
           ("ln1_rows", (2, D)), ("ln2_rows", (2, D)), ("ident_in", (P, P)), ("head_rows_in", (HEADS, HEADS, P)),
           ("causal_in", (P, P))]


def kernel(**inputs):
    import numpy as np
    import concourse.bacc as bacc
    from concourse.bass_utils import run_bass_kernel_spmd

    a = {k: np.asarray(v) for k, v in inputs.items()}
    f32 = np.float32

    def by_feature_tile(w):
        return w.reshape(KD, P, P).transpose(1, 0, 2).reshape(P, TW)

    def by_position_tile(w):
        return w.reshape(4, P, 512).transpose(1, 0, 2).reshape(P, TW)

    w_in = a["w_in"][0]
    at = {"b": 0, "c": W_CONV, "h": 2 * W_CONV, "q": 3 * W_CONV, "k": 3 * W_CONV + W_ML,
          "v": 3 * W_CONV + 2 * W_ML, "o": 3 * W_CONV + 3 * W_ML, "g": 3 * W_CONV + 4 * W_ML}
    mix = np.zeros((N_MIX, P, TW), f32)
    for n, kind in enumerate(MIX):
        if kind[0] == "gates":
            w = np.zeros((D, P), f32)
            for c in range(4):
                g = at["g"] + c % 2 * HEADS
                w[:, 32 * c:32 * c + HEADS] = w_in[:, g:g + HEADS]
            mix[n] = by_feature_tile(w)
        elif kind[0] in ("v", "o"):
            c = at[kind[0]] + kind[1] * 512
            mix[n] = by_position_tile(w_in[kind[2] * 512:kind[2] * 512 + 512, c:c + 512])
        else:
            c = at["qk"[kind[2] // 2]] + kind[1] * HD + kind[2] % 2 * P if kind[0] == "qk" \
                else at["chb"[kind[2]]] + kind[1] * P
            mix[n] = by_feature_tile(w_in[:, c:c + P])
    nf = D_FF // P
    w_up = a["w_up"][0].reshape(KD, P, 2, nf, P).transpose(3, 2, 1, 0, 4).reshape(2 * nf, P, TW)
    w_down = a["w_down"][0].reshape(GROUPS, FCH, P, 4, 512).transpose(0, 3, 2, 1, 4).reshape(nf, P, TW)
    pars = np.concatenate([a["w_ffn_conv"][0], a["b_ffn_conv"]], 0)
    ffn_conv = pars.reshape(4, 2, nf, P).transpose(3, 2, 1, 0).reshape(P, 2 * nf * 4)
    head_rows = np.zeros((HEADS, HEADS, P), f32)
    for h in range(HEADS):
        head_rows[h, h] = 1.0
    arrays = {
        "x_t": a["x"][0].T.reshape(KD, P, SEQ),
        "x_rows": a["x"][0].reshape(NS, P, D),
        "w_mix": mix, "w_out": a["w_out"][0], "w_up": w_up, "w_down": w_down,
        "b_gates": a["b_gates"][0].reshape(2, HEADS).T,
        "conv_w": a["w_sc_conv"][0].reshape(3, 8, P).transpose(2, 1, 0),
        "gain": a["mh_gain"][0].reshape(8, P).T,
        "ln1_cols": np.stack([a["ln1_g"][0], a["ln1_b"][0]]).reshape(2, KD, P).transpose(2, 0, 1),
        "ffn_conv": ffn_conv,
        "ln1_rows": np.stack([a["ln1_g"][0], a["ln1_b"][0]]),
        "ln2_rows": np.stack([a["ln2_g"][0], a["ln2_b"][0]]),
        "ident_in": np.eye(P, dtype=f32),
        "head_rows_in": head_rows,
        "causal_in": np.triu(np.ones((P, P), f32)),
    }
    nc = bacc.Bacc("TRN2", target_bir_lowering=False, num_devices=1)
    args, given = [], {}
    for name, shape in _SHAPES:
        given[name] = np.ascontiguousarray(arrays[name])
        assert given[name].shape == shape, name
        args.append(nc.dram_tensor(name, shape, F32, kind="ExternalInput").ap())
    out = nc.dram_tensor("out", (SEQ, D), F32, kind="ExternalOutput").ap()
    build(nc, *args, out)
    r = run_bass_kernel_spmd(nc, [given], core_ids=[0])
    return r.results[0]["out"].reshape(1, SEQ, D)
```
